# Optimizing a Trainium2 kernel written in Bass

```python
import jax, jax.numpy as jnp
from jax import lax
import numpy as np

D_MODEL = 2048
BATCH = 1
SEQ = 512
DEPTH = 1

CHUNK = 64
MEM_LEN = 256
D_MIX = D_MODEL
D_A = D_MIX // 2
D_B = D_MIX - D_A
A_HEADS = 8
A_HEAD_DIM = D_A // A_HEADS
SGU_BLOCK = 128
POOL_WINDOWS = (2, 4, 8, 16)
B_GROUPS = len(POOL_WINDOWS)
B_GROUP_DIM = D_B // B_GROUPS
D_IN = 2 * D_A + D_B
XATTN_HEADS = 4
XATTN_HEAD_DIM = D_MODEL // XATTN_HEADS
PEER_HEADS = 8
PEER_N_KEYS = 128
PEER_N_EXPERTS = PEER_N_KEYS * PEER_N_KEYS
PEER_TOPK = 16
PEER_D_KEY = 256
PEER_HALF = PEER_D_KEY // 2
PEER_TOKEN_BLOCK = 128
EPS = 1e-6

kernel_name = "hybrid_sgu_pool_peer_block"

def rmsnorm(x, g):
    xf = x.astype(jnp.float32)
    xf = xf * lax.rsqrt(jnp.mean(xf * xf, axis=-1, keepdims=True) + EPS)
    return xf.astype(x.dtype) * g

def layernorm(x, g, b):
    xf = x.astype(jnp.float32)
    mu = jnp.mean(xf, axis=-1, keepdims=True)
    xc = xf - mu
    xf = xc * lax.rsqrt(jnp.mean(xc * xc, axis=-1, keepdims=True) + EPS)
    return xf.astype(x.dtype) * g + b

def spatial_gating_unit(u, v, ln_g, ln_b, w_s, b_s):
    Bn, S, _ = u.shape
    nblk = S // SGU_BLOCK
    v = layernorm(v, ln_g, ln_b).reshape(Bn, nblk, SGU_BLOCK, A_HEADS, A_HEAD_DIM)
    pos = jnp.arange(SGU_BLOCK)
    mask = (pos[None, :] // CHUNK) <= (pos[:, None] // CHUNK)
    w = jnp.where(mask[None], w_s, jnp.zeros_like(w_s))
    mixed = jnp.einsum('hij,bnjhd->bnihd', w, v) + b_s.T[None, None, :, :, None]
    return u * mixed.reshape(Bn, S, D_A)

def multiscale_pool(xb, w_pool, pool_scale):
    Bn, S, _ = xb.shape
    xg = xb.reshape(Bn, S, B_GROUPS, B_GROUP_DIM)
    xf = xg.astype(jnp.float32)
    cs = jnp.cumsum(xf, axis=1)
    cs = jnp.concatenate([jnp.zeros_like(cs[:, :1]), cs], axis=1)
    t = jnp.arange(S)
    pooled = []
    for g, w in enumerate(POOL_WINDOWS):
        cs_g = cs[:, :, g]
        start = jnp.maximum(t + 1 - w, 0)
        window_sum = cs_g[:, 1:] - cs_g[:, start]
        count = (t + 1 - start).astype(jnp.float32)
        pooled.append(window_sum / count[None, :, None])
    pooled = jnp.stack(pooled, axis=2)
    y = (pooled - xf).astype(xb.dtype)
    y = jnp.einsum('bsgc,gcd->bsgd', y, w_pool)
    return y.reshape(Bn, S, D_B) * pool_scale

def memory_cross_attention(h, mem, g_q, g_mem, w_q, w_kv, w_o):
    Bn, S, D = h.shape
    n = rmsnorm(h, g_q)
    m = rmsnorm(mem, g_mem)
    q = (n @ w_q).reshape(Bn, S, XATTN_HEADS, XATTN_HEAD_DIM)
    kv = m @ w_kv
    k = kv[..., :D_MODEL].reshape(Bn, -1, XATTN_HEADS, XATTN_HEAD_DIM)
    v = kv[..., D_MODEL:].reshape(Bn, -1, XATTN_HEADS, XATTN_HEAD_DIM)
    scores = jnp.einsum('bshd,bmhd->bhsm', q, k).astype(jnp.float32) * (XATTN_HEAD_DIM ** -0.5)
    p = jax.nn.softmax(scores, axis=-1).astype(v.dtype)
    o = jnp.einsum('bhsm,bmhd->bshd', p, v).reshape(Bn, S, D)
    return o @ w_o

def peer_retrieve(n, w_query, sub_keys):
    T = n.shape[0]
    q = (n @ w_query).reshape(T, PEER_HEADS, 2, PEER_HALF)
    s = jnp.einsum('thpc,hpkc->thpk', q, sub_keys).astype(jnp.float32)
    top_s, top_i = lax.top_k(s, PEER_TOPK)
    cand_s = top_s[:, :, 0, :, None] + top_s[:, :, 1, None, :]
    cand_i = top_i[:, :, 0, :, None] * PEER_N_KEYS + top_i[:, :, 1, None, :]
    cand_s = cand_s.reshape(T, PEER_HEADS, PEER_TOPK * PEER_TOPK)
    cand_i = cand_i.reshape(T, PEER_HEADS, PEER_TOPK * PEER_TOPK)
    best_s, pos = lax.top_k(cand_s, PEER_TOPK)
    idx = jnp.take_along_axis(cand_i, pos, axis=-1)
    gates = jax.nn.softmax(best_s, axis=-1)
    return idx, gates

def peer_experts(n, idx, gates, u_table, v_table):
    T, D = n.shape
    nb = T // PEER_TOKEN_BLOCK

    def block(args):
        xb, ib, gb = args
        ue = jnp.take(u_table, ib, axis=0)
        a = jax.nn.gelu(jnp.einsum('td,thkd->thk', xb, ue), approximate=False)
        a = a * gb.astype(xb.dtype)
        ve = jnp.take(v_table, ib, axis=0)
        return jnp.einsum('thk,thkd->td', a, ve)

    out = lax.map(block, (n.reshape(nb, PEER_TOKEN_BLOCK, D),
                          idx.reshape(nb, PEER_TOKEN_BLOCK, PEER_HEADS, PEER_TOPK),
                          gates.reshape(nb, PEER_TOKEN_BLOCK, PEER_HEADS, PEER_TOPK)))
    return out.reshape(T, D)

def setup_inputs(seed: int = 0) -> dict:
    key = jax.random.key(seed)
    ks = jax.random.split(key, 24)
    f32 = jnp.float32
    D = D_MODEL

    def nrm(k, shape, scale):
        return jax.random.normal(k, shape, f32) * scale

    def gain(k, shape):
        return 1.0 + 0.05 * jax.random.normal(k, shape, f32)

    return {
        "x": nrm(ks[0], (BATCH, SEQ, D), 1.0),
        "mem": nrm(ks[1], (BATCH, MEM_LEN, D), 1.0),
        "g_mix": gain(ks[2], (DEPTH, D)),
        "w_in": nrm(ks[3], (DEPTH, D, D_IN), D ** -0.5),
        "sgu_ln_g": gain(ks[4], (DEPTH, D_A)),
        "sgu_ln_b": nrm(ks[5], (DEPTH, D_A), 0.02),
        "sgu_w": nrm(ks[6], (DEPTH, A_HEADS, SGU_BLOCK, SGU_BLOCK), 0.5 * SGU_BLOCK ** -0.5),
        "sgu_b": gain(ks[7], (DEPTH, A_HEADS, SGU_BLOCK)),
        "pool_w": nrm(ks[8], (DEPTH, B_GROUPS, B_GROUP_DIM, B_GROUP_DIM), B_GROUP_DIM ** -0.5),
        "pool_scale": 0.5 + 0.05 * jax.random.normal(ks[9], (DEPTH, D_B), f32),
        "w_out": nrm(ks[10], (DEPTH, D_MIX, D), D_MIX ** -0.5),
        "g_xattn": gain(ks[11], (DEPTH, D)),
        "g_mem": gain(ks[12], (DEPTH, D)),
        "xattn_w_q": nrm(ks[13], (DEPTH, D, D), D ** -0.5),
        "xattn_w_kv": nrm(ks[14], (DEPTH, D, 2 * D), D ** -0.5),
        "xattn_w_o": nrm(ks[15], (DEPTH, D, D), D ** -0.5),
        "g_peer": gain(ks[16], (DEPTH, D)),
        "peer_w_query": nrm(ks[17], (DEPTH, D, PEER_HEADS * PEER_D_KEY), D ** -0.5),
        "peer_sub_keys": nrm(ks[18], (DEPTH, PEER_HEADS, 2, PEER_N_KEYS, PEER_HALF), PEER_HALF ** -0.5),
        "peer_u": nrm(ks[19], (DEPTH, PEER_N_EXPERTS, D), D ** -0.5),
        "peer_v": nrm(ks[20], (DEPTH, PEER_N_EXPERTS, D), 0.7),
        "g_final": gain(ks[21], (D,)),
    }

def reference(x, mem, g_mix, w_in, sgu_ln_g, sgu_ln_b, sgu_w, sgu_b, pool_w, pool_scale, w_out,
              g_xattn, g_mem, xattn_w_q, xattn_w_kv, xattn_w_o,
              g_peer, peer_w_query, peer_sub_keys, peer_u, peer_v, g_final):
    Bn, S, D = x.shape
    h = x
    for l in range(DEPTH):
        n = rmsnorm(h, g_mix[l])
        proj = n @ w_in[l]
        u = jax.nn.gelu(proj[..., :D_A], approximate=False)
        v = jax.nn.gelu(proj[..., D_A:2 * D_A], approximate=False)
        xp = proj[..., 2 * D_A:]
        ya = spatial_gating_unit(u, v, sgu_ln_g[l], sgu_ln_b[l], sgu_w[l], sgu_b[l])
        yb = multiscale_pool(xp, pool_w[l], pool_scale[l])
        h = h + jnp.concatenate([ya, yb], axis=-1) @ w_out[l]
        h = h + memory_cross_attention(h, mem, g_xattn[l], g_mem[l],
                                       xattn_w_q[l], xattn_w_kv[l], xattn_w_o[l])
        n = rmsnorm(h, g_peer[l]).reshape(Bn * S, D)
        idx, gates = peer_retrieve(n, peer_w_query[l], peer_sub_keys[l])
        h = h + peer_experts(n, idx, gates, peer_u[l], peer_v[l]).reshape(Bn, S, D)
    return rmsnorm(h, g_final)


_drawn_inputs = setup_inputs


def setup_inputs(seed=0):
    import zlib

    import numpy as np

    out = dict(_drawn_inputs(seed))
    spreads = {}
    factors = {'sgu_ln_b': 2.915, 'g_xattn': 2.706}
    for name, (base, spread) in spreads.items():
        noise = np.random.default_rng([zlib.crc32(name.encode()), seed]).standard_normal(out[name].shape)
        drawn = base * np.exp(spread * noise) if base else spread * noise
        out[name] = __import__('jax').numpy.asarray(drawn.astype(out[name].dtype))
    for name, factor in factors.items():
        out[name] = (out[name] * factor).astype(out[name].dtype)
    return out
```

```python
from contextlib import ExitStack

import concourse.bass as bass
from concourse import mybir

F32 = mybir.dt.float32
F32R = mybir.dt.float32r
U32 = mybir.dt.uint32
ALU = mybir.AluOpType
ACT = mybir.ActivationFunctionType
AX = mybir.AxisListType.X

P = 128
D = 2048
KT = D // P
T = 512
TT = T // P
M = 256
MT = M // P
DA = 1024
NA = DA // P
XH = 4
HT = KT // XH
PH = 8
HP = 2 * PH
NK = 128
TOPK = 16
HK = PH * TOPK
NE = NK * NK
ET = NE // P
EG = 8
NG = ET // EG
DC = D // 256
EPS = 1e-6
SCALE = float(D // XH) ** -0.5
LOWEST = -3.4e38

U_KV = 0
U_IN = U_KV + 2 * KT
U_POOL = U_IN + 3 * NA
U_SGU = U_POOL + 1
U_OUT = U_SGU + 1
U_WQ = U_OUT + KT
U_WO = U_WQ + KT
U_QY = U_WO + KT
U_EU = U_QY + KT
U_EV = U_EU + ET
N_UNITS = U_EV + NG * DC

S_MEM, S_X, S_POOL, S_SGU, S_N2, S_Q, S_O, S_N3 = 0, 16, 32, 40, 48, 64, 80, 96
R_MEM, R_X, R_LNMEAN, R_LNVAR, R_N2, R_N3, R_FIN = range(7)
C_GMIX, C_GX, C_GMEM, C_GPEER, C_GFIN = 0, 16, 32, 48, 64
C_LNG, C_LNB, C_PSC, C_CNT, C_ID, C_ONE, C_IOTA = 80, 88, 96, 104, 168, 296, 424
N_CONST = 552

BANKS = 4
G_TOK = 64
G_LEAD = 8
G_ROUNDS = T // G_TOK * 2


def hybrid_block(nc, wts, xT, memT, const, bs, keys, outT):
    kv_d = nc.dram_tensor("kv_split", (2 * XH, P, 2 * HT * M), F32).ap()
    h_d = nc.dram_tensor("h_spill", (P, KT, T), F32).ap()
    act_d = nc.dram_tensor("expert_act", (ET, P, T), F32).ap()
    g_d = nc.dram_tensor("gate_matrix", (NK, P, T), F32).ap()

    base = [(nc.sbuf_base + 127) // 128 * 128]

    def region(nbytes):
        at = base[0]
        base[0] += nbytes
        return at

    def at(name, shape, dt, offset):
        return nc.alloc_sbuf_tensor_at(name, shape, dt, offset=offset)

    KB = 1024
    r_w = region(48 * KB)
    w_raw = at("w_raw", [P, 2, 2048], F32, r_w)
    w_hi = at("w_hi", [P, 2, 2048], F32R, r_w + 16 * KB)
    w_lo = at("w_lo", [P, 2, 2048], F32R, r_w + 32 * KB)

    r_a = region(64 * KB)
    a_hi = at("a_hi", [P, KT, T], F32R, r_a)
    a_lo = at("a_lo", [P, KT, T], F32R, r_a + 32 * KB)
    x_sq = at("x_sq", [P, KT, T], F32, r_a)
    ga_hi = at("ga_hi", [P, 2, EG, T], F32R, r_a)
    ga_lo = at("ga_lo", [P, 2, EG, T], F32R, r_a + 32 * KB)

    r_h = region(32 * KB)
    h = at("h", [P, KT, T], F32, r_h)
    v_fm = at("v_fm", [P, NA, T], F32, r_h)
    pad = [at(f"pad{n}", [P, 16 + T], F32, r_h + 16 * KB + 2112 * n) for n in range(3)]
    y_raw = at("y_raw", [P, 3, T], F32, r_h + 16 * KB + 6336)
    ln_st = at("ln_st", [P, T], F32, r_h + 16 * KB + 12480)
    vt_lo = at("vt_lo", [P, TT, DA], F32R, r_h + 16 * KB)
    e_act = at("e_act", [P, 4, T], F32, r_h)
    i_T = at("i_T", [P, T], F32, r_h + 8 * KB)
    j_T = at("j_T", [P, T], F32, r_h + 10 * KB)
    gt_hi = at("gt_hi", [P, T], F32R, r_h + 12 * KB)
    gt_lo = at("gt_lo", [P, T], F32R, r_h + 14 * KB)
    oh_i = at("oh_i", [P, 8, P], F32R, r_h + 16 * KB)
    oh_jh = at("oh_jh", [P, 8, P], F32R, r_h + 20 * KB)
    oh_jl = at("oh_jl", [P, 8, P], F32R, r_h + 24 * KB)

    r_q = region(32 * KB)
    mem_raw = at("mem_raw", [P, KT, M], F32, r_q)
    mem_sq = at("mem_sq", [P, KT, M], F32, r_q + 16 * KB)
    kv_out = at("kv_out", [P, XH, 2, HT * M], F32R, r_q)
    vt_hi = at("vt_hi", [P, TT, DA], F32R, r_q)
    u_act = at("u_act", [P, NA, T], F32, r_q + 16 * KB)
    q_raw = at("q_raw", [P, KT, T], F32, r_q)
    prob = at("prob", [P, 2, TT, M], F32, r_q)
    pt_hi = at("pt_hi", [P, 2, MT, T], F32R, r_q + 8 * KB)
    pt_lo = at("pt_lo", [P, 2, MT, T], F32R, r_q + 16 * KB)
    key_raw = at("key_raw", [P, HP, NK], F32, r_q)
    score = at("score", [P, TT, HP, NK], F32, r_q)
    ag = at("ag", [P, 2, 2, 4, T], F32, r_q)

    r_k = region(32 * KB)
    m_hi = at("m_hi", [P, KT, M], F32R, r_k)
    m_lo = at("m_lo", [P, KT, M], F32R, r_k + 16 * KB)
    y_hi = at("y_hi", [P, NA, T], F32R, r_k)
    y_lo = at("y_lo", [P, NA, T], F32R, r_k + 16 * KB)
    k_in = at("k_in", [P, 2, 2, HT, M], F32R, r_k)
    v_in = at("v_in", [P, 2, 2, MT, 512], F32R, r_k + 16 * KB)
    key_hi = at("key_hi", [P, HP, NK], F32R, r_k)
    key_lo = at("key_lo", [P, HP, NK], F32R, r_k + 8 * KB)
    qy_hi = at("qy_hi", [P, 2, T], F32R, r_k + 16 * KB)
    qy_lo = at("qy_lo", [P, 2, T], F32R, r_k + 20 * KB)
    s_w = at("s_w", [P, HP, NK], F32, r_k)
    s_w2 = at("s_w2", [P, HP, NK], F32, r_k + 8 * KB)
    cand = at("cand", [P, PH, 256], F32, r_k + 16 * KB)
    cand2 = at("cand2", [P, PH, 256], F32, r_k)
    match = at("match", [P, HK, 16], F32, r_k + 8 * KB)
    top_v = at("top_v", [P, HP, 16], F32, r_k + 24 * KB)
    top_i = at("top_i", [P, HP, 16], U32, r_k + 25 * KB)
    top_f = at("top_f", [P, HP, 16], F32, r_k + 26 * KB)
    best = at("best", [P, PH, 16], F32, r_k + 27 * KB)
    pos = at("pos", [P, PH, 16], U32, r_k + 27 * KB + 512)
    pos_ab = at("pos_ab", [P, 2, HK], U32, r_k + 28 * KB)
    pos_f = at("pos_f", [P, 2, HK], F32, r_k + 29 * KB)
    g_out = at("g_out", [P, 2, NK, G_TOK], F32, r_q)

    rms = at("rms", [P, T], F32, region(2 * KB))
    acc = at("acc", [P, T], F32, region(2 * KB))
    sq = at("sq", [P, T], F32, region(2 * KB))
    r_s = region(6 * KB)
    kv_raw = at("kv_raw", [P, 4, M], F32, r_s)
    bias_s = at("bias_s", [P, NA, P], F32, r_s)
    stat = at("stat", [P, 3, XH, TT], F32, r_s)
    pick = at("pick", [P, 3, TT, HK], F32, r_s)
    gsum = at("gsum", [P, 2, TT * PH], F32, region(256))
    cst = at("cst", [P, N_CONST], F32, region(4 * N_CONST))
    assert base[0] <= nc.sbuf_usable_end, base[0]

    ident = cst[:, C_ID:C_ID + P]
    ones = cst[:, C_ONE:C_ONE + P]
    iota = cst[:, C_IOTA:C_IOTA + P]

    ctx = ExitStack()
    with ctx:
        ps = [ctx.enter_context(nc.psum_tensor(f"ps{n}", [P, 512], F32)) for n in range(8)]

        def sem(name):
            return ctx.enter_context(nc.semaphore(name))

        w_landed = [sem("w_landed0"), sem("w_landed1")]
        w_hi_ok, w_lo_ok = sem("w_hi_ok"), sem("w_lo_ok")
        unit_done = sem("unit_done")
        evac = sem("evac")
        mv_hi, mv_lo = sem("mv_hi"), sem("mv_lo")
        mem_in, x_in, x_back, cst_in, bias_in, key_in = (
            sem("mem_in"), sem("x_in"), sem("x_back"), sem("cst_in"), sem("bias_in"), sem("key_in"))
        sq_ok = sem("sq_ok")
        st_in, st_ps, st_ms, st_rt = sem("st_in"), sem("st_ps"), sem("st_ms"), sem("st_rt")
        chain = sem("chain")
        kv_ok, kvh_ok, kvl_ok = sem("kv_ok"), sem("kvh_ok"), sem("kvl_ok")
        kv_store = sem("kv_store")
        vT_ok = sem("vT_ok")
        v_ok, v_gelu, v_norm = sem("v_ok"), sem("v_gelu"), sem("v_norm")
        y_ok, yh_ok, yl_ok = sem("y_ok"), sem("yh_ok"), sem("yl_ok")
        vtt_ok, vth_ok, vtl_ok = sem("vtt_ok"), sem("vth_ok"), sem("vtl_ok")
        u_ok, u_gelu = sem("u_ok"), sem("u_gelu")
        pool_ps, sgu_ps, sgu_y = sem("pool_ps"), sem("sgu_ps"), sem("sgu_y")
        h_ok, hs_ok, acc_ok = sem("h_ok"), sem("hs_ok"), sem("acc_ok")
        q_ok = sem("q_ok")
        k_land = [sem("k_land0"), sem("k_land1")]
        v_land = [sem("v_land0"), sem("v_land1")]
        sc_ps, mx_ok, ex_ok, pn_ok = sem("sc_ps"), sem("mx_ok"), sem("ex_ok"), sem("pn_ok")
        pT_ps, pth_ok, ptl_ok, o_ps = sem("pT_ps"), sem("pth_ok"), sem("ptl_ok"), sem("o_ps")
        keyh_ok, keyl_ok = sem("keyh_ok"), sem("keyl_ok")
        qyh_ok, qs_ps, qs_ok = sem("qyh_ok"), sem("qs_ps"), sem("qs_ok")
        h_out, h_back = sem("h_out"), sem("h_back")
        ea_ok = sem("ea_ok")
        ea_out = [sem(f"ea_out{n}") for n in range(4)]
        tk = sem("tk")
        tk_seen = sem("tk_seen")
        gexp_in, gexp_ok = sem("gexp_in"), sem("gexp_ok")
        pick_ok, pick_ps, idx_ok = sem("pick_ok"), sem("pick_ps"), sem("idx_ok")
        oh_ok, g_ps, g_ok = sem("oh_ok"), sem("g_ps"), sem("g_ok")
        g_st = [sem("g_st0"), sem("g_st1")]
        ag_in = [sem("ag_in0"), sem("ag_in1")]
        am_ok, ah_ok, al_ok = sem("am_ok"), sem("ah_ok"), sem("al_ok")
        add_ok = sem("add_ok")
        o_ok, o_st = sem("o_ok"), sem("o_st")

        block = ctx.enter_context(nc.Block())

        @block.sync
        def _(sp):
            def load_unit(u, slot, first=False):
                if not first:
                    sp.wait_ge(w_lo_ok, u * 2 - 2)
                src = wts[u] if isinstance(u, int) else wts[bass.ds(u, 1)].rearrange("a p n -> (a p) n")
                sp.dma_start(w_raw[:, slot], src).then_inc(w_landed[slot], 16)

            def load_units(u0, n):
                with sp.Fori(0, n // 2) as i:
                    load_unit(i * 2 + u0, 0)
                    load_unit(i * 2 + (u0 + 1), 1)

            sp.dma_start(cst[:, :], const).then_inc(cst_in, 16)
            sp.dma_start(mem_raw[:, :, :], memT).then_inc(mem_in, 16)
            load_unit(0, 0, True)
            load_unit(1, 1, True)
            sp.dma_start(h[:, :, :], xT).then_inc(x_in, 16)
            load_units(2, U_IN - 2)
            load_units(U_IN, 4)
            sp.wait_ge(kvl_ok, 2 * KT)
            sp.dma_start(bias_s[:, :, :], bs).then_inc(bias_in, 16)
            load_units(U_IN + 4, U_OUT - U_IN - 4)
            load_units(U_OUT, 2)
            sp.wait_ge(sgu_ps, NA)
            sp.dma_start(h[:, :, :], xT).then_inc(x_back, 16)
            load_units(U_OUT + 2, KT - 2)

            def load_kv(head):
                s = head % 2
                if head == 0:
                    sp.wait_ge(pool_ps, NA)
                    sp.wait_ge(kv_store, 16 * 2 * XH)
                if head >= 2:
                    sp.wait_ge(sc_ps, head - 1)
                sp.dma_start(k_in[:, s].rearrange("p a t m -> p (a t m)").bitcast(F32), kv_d[head]).then_inc(k_land[s], 16)
                if head >= 2:
                    sp.wait_ge(o_ps, HT * (head - 1))
                sp.dma_start(v_in[:, s].rearrange("p a t m -> p (a t m)").bitcast(F32), kv_d[XH + head]).then_inc(v_land[s], 16)

            load_kv(0)
            load_kv(1)
            load_units(U_WQ, KT + 2)
            load_kv(2)
            load_kv(3)
            sp.wait_ge(o_ps, XH * HT)
            sp.dma_start(key_raw[:, :, :], keys).then_inc(key_in, 16)
            load_units(U_WO + 2, 2 * KT - 2)
            load_units(U_EU, ET + 2)
            sp.wait_ge(h_out, 16)
            for s in range(4):
                sp.wait_ge(ea_out[s], 16 * (ET // 4))
            sp.wait_ge(idx_ok, 4)
            sp.wait_ge(g_ps, T // 4)
            sp.dma_start(h[:, :, :], h_d).then_inc(h_back, 16)
            for s in range(2):
                sp.wait_ge(g_st[s], 16 * (T // G_TOK // 2))

            def load_ag(m, first=False):
                for s in range(2):
                    mm = m * 2 + s
                    if not first:
                        sp.wait_ge(al_ok, mm * 4 - 4)
                    for n, src in enumerate((act_d, g_d)):
                        if isinstance(mm, int):
                            part = src[mm * 4:mm * 4 + 4]
                        else:
                            part = src[bass.ds(mm * 4, 4)]
                        sp.dma_start(ag[:, s, n], part.rearrange("e p t -> p e t")).then_inc(ag_in[s], 16)

            load_ag(0, True)
            with sp.Fori(0, NG - 1) as g:
                for c in range(0, DC, 2):
                    load_unit(g * DC + (U_EV + 2 + c), 0)
                    load_unit(g * DC + (U_EV + 3 + c), 1)
                    if c == 0:
                        load_ag(g + 1)
            for u in range(N_UNITS - DC + 2, N_UNITS):
                load_unit(u, u % 2)
            for k in range(0, KT, 4):
                sp.wait_ge(o_ok, k + 4)
                sp.dma_start(outT[:, k:k + 4], h[:, k:k + 4]).then_inc(o_st, 16)
            sp.wait_ge(o_st, 16 * (KT // 4))

        @block.gpsimd
        def _(pool):
            with pool.Fori(0, N_UNITS // 2) as i:
                for s in range(2):
                    for half in range(2):
                        pool.wait_ge(w_hi_ok, i * 4 + (2 * s + half + 1))
                        c = slice(half * 1024, half * 1024 + 1024)
                        pool.tensor_tensor(w_lo[:, s, c], w_raw[:, s, c], w_hi[:, s, c].bitcast(F32),
                                           ALU.subtract).then_inc(w_lo_ok, 1)

        @block.scalar
        def _(act):
            def w_high(i, c, first=False):
                s = c % 2
                act.wait_ge(w_landed[s], i * 16 + (c // 2 * 16 + 16))
                if not first:
                    act.wait_ge(unit_done, i * 2 + (c - 1))
                for half in range(2):
                    cc = slice(half * 1024, half * 1024 + 1024)
                    act.activation(w_hi[:, s, cc], w_raw[:, s, cc], ACT.Copy).then_inc(w_hi_ok, 1)

            def units(u0, n, post, extra=None):
                assert u0 % 2 == 0 and n % 2 == 0
                with act.Fori(0, (n - 2) // 2) as r:
                    for k in range(2):
                        w_high(r, u0 + 2 + k)
                        post(r * 2 + k, k)
                w_high(0, u0 + n)
                post(n - 2, 0)
                post(n - 1, 1)

            def resume(u0):
                w_high(0, u0 + 1)

            def sqrt_of(count, t, cols):
                act.wait_ge(st_ms, count)
                act.activation(t[:, 0:cols], t[:, 0:cols], ACT.Sqrt).then_inc(st_rt, 1)

            act.wait_ge(cst_in, 16)
            act.wait_ge(mem_in, 16)
            act.activation(mem_sq[:, :, :], mem_raw[:, :, :], ACT.Square).then_inc(sq_ok, 1)
            for k in range(KT):
                act.activation(m_hi[:, k], mem_raw[:, k], ACT.Copy,
                               scale=cst[:, C_GMEM + k:C_GMEM + k + 1]).then_inc(mv_hi, 1)
                if k == 3:
                    w_high(0, 0, True)
            w_high(0, 1, True)
            sqrt_of(1, rms, M)
            act.wait_ge(x_in, 16)
            act.activation(x_sq[:, :, :], h[:, :, :], ACT.Square).then_inc(sq_ok, 1)

            with act.Fori(0, XH) as r:
                for k in range(HT):
                    w_high(r * 2, U_KV + 2 + k)
                    act.wait_ge(kv_ok, r * HT + (k + 1))
                    if k == 0:
                        act.wait_ge(mv_lo, KT)
                    act.activation(kv_out[:, bass.ds(r, 1), 0, k * M:(k + 1) * M], kv_raw[:, k:k + 1],
                                   ACT.Copy).then_inc(kvh_ok, 1)
                act.wait_ge(kvl_ok, r * HT + HT)
                act.dma_start(kv_d[bass.ds(r, 1)].rearrange("a p n -> p (a n)"),
                              kv_out[:, bass.ds(r, 1)].rearrange("p a s n -> p (a s n)").bitcast(F32)).then_inc(kv_store, 16)
            act.wait_ge(kv_store, 16 * XH)

            act.wait_ge(st_in, R_X + 1)
            for k in range(KT):
                act.activation(a_hi[:, k], h[:, k], ACT.Copy,
                               scale=cst[:, C_GMIX + k:C_GMIX + k + 1]).then_inc(mv_hi, 1)
                if k == 7:
                    w_high(0, U_KV + KT + 2)

            def v_high(r, k):
                act.wait_ge(vT_ok, r * HT + (k + 1))
                act.activation(kv_out[:, bass.ds(r, 1), 0].rearrange("p a (t n) -> p (a t) n", t=MT)[:, :, k * P:(k + 1) * P],
                               ps[4 + k][:, 0:M].rearrange("p (t n) -> p t n", t=MT), ACT.Copy).then_inc(kvh_ok, 1)

            with act.Fori(0, XH) as r:
                for k in range(HT):
                    if k:
                        w_high(r * 2, U_KV + KT + 2 + k)
                        v_high(r, k - 1)
                v_high(r, HT - 1)
                act.wait_ge(kvl_ok, r * HT + (KT + HT))
                act.dma_start(kv_d[bass.ds(r + XH, 1)].rearrange("a p n -> p (a n)"),
                              kv_out[:, bass.ds(r, 1)].rearrange("p a s n -> p (a s n)").bitcast(F32)).then_inc(kv_store, 16)
                w_high(r * 2, U_KV + KT + 2 + HT)
            sqrt_of(2, rms, T)
            w_high(0, U_IN + 3)
            act.wait_ge(kv_store, 16 * 2 * XH)

            for i in range(NA):
                act.wait_ge(v_ok, i + 1)
                act.activation(v_fm[:, i], v_fm[:, i], ACT.Gelu).then_inc(v_gelu, 1)
                if i < NA - 1:
                    w_high(0, U_IN + 4 + i)
            for i in range(NA):
                w_high(0, U_IN + NA + 3 + i)
                act.wait_ge(y_ok, i + 1)
                act.activation(y_hi[:, i], y_raw[:, i % 3], ACT.Copy).then_inc(yh_ok, 1)
            sqrt_of(3, ln_st, T)
            for i in range(NA):
                act.wait_ge(u_ok, i + 1)
                act.activation(u_act[:, i], u_act[:, i], ACT.Gelu).then_inc(u_gelu, 1)
                if i == 3:
                    for n in range(2 * TT):
                        act.wait_ge(vtt_ok, n + 1)
                        t, c = n // 2, n % 2
                        act.activation(vt_hi[:, t, c * 512:c * 512 + 512], ps[4 + n % 4][:, :],
                                       ACT.Copy).then_inc(vth_ok, 1)
                if i < NA - 1:
                    w_high(0, U_IN + 2 * NA + 3 + i)
            for o in range(NA):
                act.wait_ge(pool_ps, o + 1)
                if o == 0:
                    act.wait_ge(unit_done, U_POOL)
                act.activation(a_hi[:, NA + o], ps[4 + o % 4][:, :], ACT.Copy,
                               scale=cst[:, C_PSC + o:C_PSC + o + 1]).then_inc(mv_hi, 1)
            w_high(0, U_OUT)
            for o in range(NA):
                act.wait_ge(sgu_y, o + 1)
                act.activation(a_hi[:, o], u_act[:, o], ACT.Copy).then_inc(mv_hi, 1)
            w_high(0, U_OUT + 1)

            def nothing(i, k):
                pass

            def scaled_high(gain, end):
                act.wait_ge(unit_done, end)
                for k in range(KT):
                    act.activation(a_hi[:, k], h[:, k], ACT.Copy,
                                   scale=cst[:, gain + k:gain + k + 1]).then_inc(mv_hi, 1)
                    if k == 7:
                        resume(end)

            units(U_OUT, KT, nothing)
            act.wait_ge(h_ok, KT)
            scaled_high(C_GX, U_WQ)
            sqrt_of(4, rms, T)
            units(U_WQ, KT, nothing)

            act.wait_ge(unit_done, U_WO)
            for k in range(KT):
                act.wait_ge(q_ok, k + 1)
                act.activation(a_hi[:, k], q_raw[:, k], ACT.Copy).then_inc(mv_hi, 1)
            act.wait_ge(mv_lo, S_Q + KT)

            def exps(head):
                act.wait_ge(mx_ok, head + 1)
                if head >= 2:
                    act.wait_ge(pT_ps, head - 1)
                for t in range(TT):
                    act.activation(prob[:, head % 2, t],
                                   ps[4 + 2 * (head % 2) + t // 2][:, (t % 2) * M:(t % 2 + 1) * M], ACT.Exp,
                                   bias=stat[:, 0, head, t:t + 1], scale=SCALE,
                                   accum_out=stat[:, 1, head, t:t + 1]).then_inc(ex_ok, 1)

            exps(0)
            for head in range(XH):
                act.wait_ge(pT_ps, head + 1)
                if head >= 2:
                    act.wait_ge(o_ps, HT * (head - 1))
                for m in range(MT):
                    act.activation(pt_hi[:, head % 2, m], ps[m][:, :], ACT.Copy).then_inc(pth_ok, 1)
                if head + 1 < XH:
                    exps(head + 1)
                for n in range(HT):
                    o = head * HT + n
                    act.wait_ge(o_ps, o + 1)
                    act.activation(a_hi[:, o], ps[2 + o % 2][:, :], ACT.Copy).then_inc(mv_hi, 1)
            resume(U_WO)
            act.wait_ge(key_in, 16)
            act.activation(key_hi[:, :, :], key_raw[:, :, :], ACT.Copy).then_inc(keyh_ok, 1)

            units(U_WO, KT, nothing)
            sqrt_of(5, rms, T)
            for k in range(KT):
                act.wait_ge(h_ok, 2 * KT + k + 1)
                act.activation(a_hi[:, k], q_raw[:, k], ACT.Copy).then_inc(mv_hi, 1)
                if k == 7:
                    resume(U_QY)
            act.dma_start(h_d, h[:, :, :]).then_inc(h_out, 16)

            act.sem_inc(qs_ok, BANKS)
            act.wait_ge(mv_lo, S_N3 + KT)

            def query_high(r, k):
                act.wait_ge(unit_done, r * 4 + (U_QY + k + 1))
                act.wait_ge(qs_ps, r * 4 + (k + 2))
                act.activation(qy_hi[:, k % 2], ps[k][:, :], ACT.Copy).then_inc(qyh_ok, 1)

            def score_copy(r, k):
                act.wait_ge(qs_ps, r * 4 + (k + 4))
                act.activation(score[:, :, bass.ds(r * 4 + k, 1), :],
                               ps[4 + k][:, :].rearrange("p (t a n) -> p t a n", t=TT, a=1),
                               ACT.Copy).then_inc(qs_ok, 1)

            with act.Fori(0, KT // 4) as r:
                for k in range(4):
                    w_high(r * 2, U_QY + 2 + k)
                    query_high(r, k)
                    if k:
                        score_copy(r, k - 1)
                score_copy(r, 3)

            act.wait_ge(h_out, 16)

            def u_round(r):
                for k in range(4):
                    w_high(r * 2, U_EU + 2 + k)
                    act.wait_ge(unit_done, r * 4 + (U_EU + k + 1))
                    if not (isinstance(r, int) and r == 0):
                        act.wait_ge(ea_out[k], r * 16)
                    act.activation(e_act[:, k], ps[k][:, :], ACT.Gelu).then_inc(ea_ok, 1)
                    act.wait_ge(ea_ok, r * 4 + (BANKS + k + 1))
                    dst = act_d[r * 4 + k] if isinstance(r, int) else act_d[bass.ds(r * 4 + k, 1)].rearrange("a p t -> (a p) t")
                    act.dma_start(dst, e_act[:, k]).then_inc(ea_out[k], 16)

            act.sem_inc(ea_ok, BANKS)
            u_round(0)
            with act.Fori(1, G_LEAD) as r:
                u_round(r)
            act.wait_ge(gexp_in, 1)
            act.activation(pick[:, 2], pick[:, 2], ACT.Exp).then_inc(gexp_ok, 1)

            def g_copy(b, n, slot):
                act.wait_ge(g_ps, b + (n + 1))
                col = (n % 16) * 4
                act.activation(g_out[:, slot, :, col:col + 4].rearrange("p i t -> p t i"),
                               ps[4 + n % 4][:, :].rearrange("p (t i) -> p t i", t=4), ACT.Copy).then_inc(g_ok, 1)

            def g_rounds(q):
                for slot in range(2):
                    for b in range(2):
                        u_round(q * 4 + (G_LEAD + 2 * slot + b))
                        for n in range(8):
                            if b == 0 and n == 0 and not (isinstance(q, int) and q == 0):
                                act.wait_ge(g_st[slot], q * 16)
                            g_copy(q * 32 + slot * 16, b * 8 + n, slot)
                    act.wait_ge(g_ok, q * 32 + (slot * 16 + 16))
                    if isinstance(q, int):
                        dst = g_d[:, :, (q * 2 + slot) * G_TOK:(q * 2 + slot + 1) * G_TOK]
                    else:
                        dst = g_d[:, :, bass.ds(q * (2 * G_TOK) + slot * G_TOK, G_TOK)]
                    act.dma_start(dst.rearrange("i p t -> p i t"), g_out[:, slot]).then_inc(g_st[slot], 16)

            g_rounds(0)
            with act.Fori(1, G_ROUNDS // 4) as q:
                g_rounds(q)
            with act.Fori(G_LEAD + G_ROUNDS, ET // 4) as r:
                u_round(r)

            def gated_high(m, buf, n):
                act.wait_ge(am_ok, m * EG + (n + 1))
                act.activation(ga_hi[:, buf, n], ag[:, n // 4, 0, n % 4], ACT.Copy).then_inc(ah_ok, 1)

            act.wait_ge(unit_done, U_EV)
            for n in range(EG):
                gated_high(0, 0, n)

            def v_group(g2, b, prep=True, ends=False):
                for c in range(DC):
                    u = U_EV + b * DC + c + 2
                    if not (ends and c >= DC - 2):
                        w_high(g2 * DC, u)
                    if prep:
                        gated_high(g2 * 2 + (b + 1), 1 - b, c)

            with act.Fori(0, NG // 2 - 1) as g2:
                v_group(g2, 0)
                v_group(g2, 1)
            v_group(NG // 2 - 1, 0)
            v_group(NG // 2 - 1, 1, prep=False, ends=True)
            sqrt_of(6, rms, T)

        @block.vector
        def _(dve):
            steps = [0]

            def link(ins):
                steps[0] += 1
                ins.then_inc(chain, 1)
                dve.wait_ge(chain, steps[0])

            def low(out, src, hi, gain=None):
                if gain is None:
                    ins = dve.tensor_tensor(out, src, hi.bitcast(F32), ALU.subtract)
                else:
                    ins = dve.scalar_tensor_tensor(out, src, cst[:, gain:gain + 1], hi.bitcast(F32),
                                                   ALU.mult, ALU.subtract)
                return ins

            def mean_from(n, t, cols, width, eps):
                dve.wait_ge(st_ps, n + 1)
                return dve.tensor_scalar(t[:, 0:cols], ps[7][:, 0:cols], 1.0 / width, eps, ALU.mult, ALU.add)

            def rsqrt_from(n, count, t, cols, width):
                mean_from(n, t, cols, width, EPS).then_inc(st_ms, 1)
                dve.wait_ge(st_rt, count)
                link(dve.reciprocal(t[:, 0:cols], t[:, 0:cols]))

            def evacuated(u):
                dve.wait_ge(unit_done, u + 1)

            dve.sem_inc(evac, BANKS)
            dve.wait_ge(cst_in, 16)
            dve.wait_ge(sq_ok, 1)
            dve.tensor_reduce(acc[:, 0:M], mem_sq[:, :, :].rearrange("p k t -> p t k"), AX, ALU.add).then_inc(st_in, 1)
            for k in range(KT):
                dve.wait_ge(mv_hi, S_MEM + k + 1)
                low(m_lo[:, k], mem_raw[:, k], m_hi[:, k], C_GMEM + k).then_inc(mv_lo, 1)
            rsqrt_from(R_MEM, 1, rms, M, D)
            def kv_scale(r, k, u0, n0):
                evacuated(r * 4 + (u0 + k))
                dve.tensor_tensor(kv_raw[:, k], ps[k][:, 0:M], rms[:, 0:M], ALU.mult).then_inc(kv_ok, 1)
                dve.wait_ge(kv_ok, r * 4 + (n0 + k + 1))
                dve.sem_inc(evac, 1)

            with dve.Fori(0, XH) as r:
                for k in range(HT):
                    kv_scale(r, k, U_KV, 0)
                    dve.wait_ge(kvh_ok, r * 4 + (k + 1))
                    low(kv_out[:, bass.ds(r, 1), 1, k * M:(k + 1) * M], kv_raw[:, k:k + 1],
                        kv_out[:, bass.ds(r, 1), 0, k * M:(k + 1) * M]).then_inc(kvl_ok, 1)
            dve.wait_ge(sq_ok, 2)
            dve.tensor_reduce(acc[:, :], x_sq[:, :, :].rearrange("p k t -> p t k"), AX, ALU.add).then_inc(st_in, 1)
            for k in range(KT):
                dve.wait_ge(mv_hi, S_X + k + 1)
                low(a_lo[:, k], h[:, k], a_hi[:, k], C_GMIX + k).then_inc(mv_lo, 1)
            def v_low(r, k):
                dve.wait_ge(kvh_ok, r * 4 + (KT + k + 1))
                low(kv_out[:, bass.ds(r, 1), 1].rearrange("p a (t n) -> p (a t) n", t=MT)[:, :, k * P:(k + 1) * P],
                    ps[4 + k][:, 0:M].rearrange("p (t n) -> p t n", t=MT),
                    kv_out[:, bass.ds(r, 1), 0].rearrange("p a (t n) -> p (a t) n", t=MT)[:, :, k * P:(k + 1) * P]
                    ).then_inc(kvl_ok, 1)

            with dve.Fori(0, XH) as r:
                for k in range(HT):
                    kv_scale(r, k, U_KV + KT, KT)
                    if k:
                        v_low(r, k - 1)
                v_low(r, HT - 1)

            rsqrt_from(R_X, 2, rms, T, D)
            for i in range(NA):
                evacuated(U_IN + i)
                dve.tensor_tensor(v_fm[:, i], ps[i % 4][:, :], rms[:, :], ALU.mult).then_inc(v_ok, 1)
                dve.wait_ge(v_ok, i + 1)
                dve.sem_inc(evac, 1)
                dve.wait_ge(v_gelu, i + 1)
                if i == 1:
                    link(dve.tensor_tensor(acc[:, :], v_fm[:, 0], v_fm[:, 1], ALU.add))
                elif i > 1:
                    link(dve.tensor_tensor(acc[:, :], acc[:, :], v_fm[:, i], ALU.add))
            dve.sem_inc(st_in, 1)
            for t in pad:
                link(dve.memset(t[:, 0:16], 0.0))

            def pooled(i):
                w = 2 << (i // 2)
                evacuated(U_IN + NA + i)
                x = pad[0]
                link(dve.tensor_tensor(x[:, 16:16 + T], ps[i % 4][:, :], rms[:, :], ALU.mult))
                dve.sem_inc(evac, 1)
                src, n, s = x, 1, 1
                while s < w:
                    dst = pad[n]
                    link(dve.tensor_tensor(dst[:, 16:16 + T], src[:, 16:16 + T], src[:, 16 - s:16 - s + T], ALU.add))
                    src, n, s = dst, 3 - n, 2 * s
                y = y_raw[:, i % 3]
                if i >= 3:
                    dve.wait_ge(yh_ok, i - 2)
                link(dve.tensor_tensor(y[:, 0:16], src[:, 16:32], cst[:, C_CNT + 16 * (i // 2):C_CNT + 16 * (i // 2) + 16], ALU.mult))
                dve.tensor_tensor(y[:, 0:16], y[:, 0:16], x[:, 16:32], ALU.subtract)
                dve.scalar_tensor_tensor(y[:, 16:T], src[:, 32:16 + T], 1.0 / w, x[:, 32:16 + T],
                                         ALU.mult, ALU.subtract).then_inc(y_ok, 1)
                dve.wait_ge(yh_ok, i + 1)
                low(y_lo[:, i], y, y_hi[:, i]).then_inc(yl_ok, 1)

            for i in range(4):
                pooled(i)
            link(mean_from(R_LNMEAN, ln_st, T, DA, 0.0))
            for i in range(NA):
                link(dve.tensor_tensor(v_fm[:, i], v_fm[:, i], ln_st[:, :], ALU.subtract))
                if i == 0:
                    link(dve.tensor_tensor(acc[:, :], v_fm[:, i], v_fm[:, i], ALU.mult))
                else:
                    link(dve.tensor_tensor(sq[:, :], v_fm[:, i], v_fm[:, i], ALU.mult))
                    link(dve.tensor_tensor(acc[:, :], acc[:, :], sq[:, :], ALU.add))
            dve.sem_inc(st_in, 1)
            for i in range(4, NA):
                pooled(i)
            rsqrt_from(R_LNVAR, 3, ln_st, T, DA)
            for i in range(NA):
                link(dve.tensor_tensor(v_fm[:, i], v_fm[:, i], ln_st[:, :], ALU.mult))
                dve.tensor_scalar(v_fm[:, i], v_fm[:, i], cst[:, C_LNG + i:C_LNG + i + 1],
                                  cst[:, C_LNB + i:C_LNB + i + 1], ALU.mult, ALU.add).then_inc(v_norm, 1)
            for i in range(NA):
                evacuated(U_IN + 2 * NA + i)
                dve.tensor_tensor(u_act[:, i], ps[i % 4][:, :], rms[:, :], ALU.mult).then_inc(u_ok, 1)
                dve.wait_ge(u_ok, i + 1)
                dve.sem_inc(evac, 1)
                if i == 3:
                    for n in range(2 * TT):
                        dve.wait_ge(vth_ok, n + 1)
                        t, c = n // 2, n % 2
                        low(vt_lo[:, t, c * 512:c * 512 + 512], ps[4 + n % 4][:, :],
                            vt_hi[:, t, c * 512:c * 512 + 512]).then_inc(vtl_ok, 1)
            for o in range(NA):
                dve.wait_ge(mv_hi, S_POOL + o + 1)
                low(a_lo[:, NA + o], ps[4 + o % 4][:, :], a_hi[:, NA + o], C_PSC + o).then_inc(mv_lo, 1)
            dve.wait_ge(bias_in, 16)
            dve.wait_ge(u_gelu, NA)
            for o in range(NA):
                dve.wait_ge(sgu_ps, o + 1)
                mixed = ps[4 + o % 4][:, :].rearrange("p (b i) -> p b i", b=TT)
                link(dve.tensor_tensor(sq[:, :].rearrange("p (b i) -> p b i", b=TT), mixed,
                                       bias_s[:, o:o + 1, :].to_broadcast([P, TT, P]), ALU.add))
                dve.tensor_tensor(u_act[:, o], u_act[:, o], sq[:, :], ALU.mult).then_inc(sgu_y, 1)
                dve.wait_ge(mv_hi, S_SGU + o + 1)
                low(a_lo[:, o], u_act[:, o], a_hi[:, o]).then_inc(mv_lo, 1)

            def residual(u0, n0):
                link(dve.memset(acc[:, :], 0.0))
                with dve.Fori(0, KT // 4) as r:
                    for k in range(4):
                        evacuated(r * 4 + (u0 + k))
                        hk = h[:, bass.ds(r * 4 + k, 1), :].rearrange("p a t -> p (a t)")
                        dve.tensor_tensor(hk, hk, ps[k][:, :], ALU.add).then_inc(h_ok, 1)
                        dve.wait_ge(h_ok, r * 4 + (n0 + k + 1))
                        dve.sem_inc(evac, 1)
                        dve.tensor_tensor(sq[:, :], hk, hk, ALU.mult).then_inc(hs_ok, 1)
                        dve.wait_ge(hs_ok, r * 4 + (n0 + k + 1))
                        dve.tensor_tensor(acc[:, :], acc[:, :], sq[:, :], ALU.add).then_inc(acc_ok, 1)
                dve.wait_ge(acc_ok, n0 + KT)
                dve.sem_inc(st_in, 1)

            dve.wait_ge(x_back, 16)
            residual(U_OUT, 0)
            for k in range(KT):
                dve.wait_ge(mv_hi, S_N2 + k + 1)
                low(a_lo[:, k], h[:, k], a_hi[:, k], C_GX + k).then_inc(mv_lo, 1)
            rsqrt_from(R_N2, 4, rms, T, D)
            with dve.Fori(0, KT // 4) as r:
                for k in range(4):
                    evacuated(r * 4 + (U_WQ + k))
                    dve.tensor_tensor(q_raw[:, bass.ds(r * 4 + k, 1), :].rearrange("p a t -> p (a t)"),
                                      ps[k][:, :], rms[:, :], ALU.mult).then_inc(q_ok, 1)
                    dve.wait_ge(q_ok, r * 4 + (k + 1))
                    dve.sem_inc(evac, 1)
            for k in range(KT):
                dve.wait_ge(mv_hi, S_Q + k + 1)
                low(a_lo[:, k], q_raw[:, k], a_hi[:, k]).then_inc(mv_lo, 1)

            def maxima(head):
                dve.wait_ge(sc_ps, head + 1)
                for b in range(2):
                    link(dve.tensor_reduce(stat[:, 0, head, 2 * b:2 * b + 2],
                                           ps[4 + 2 * (head % 2) + b][:, :].rearrange("p (t m) -> p t m", t=2), AX, ALU.max))
                dve.tensor_scalar(stat[:, 0, head], stat[:, 0, head], -SCALE, None, ALU.mult).then_inc(mx_ok, 1)

            def normalised(head):
                dve.wait_ge(ex_ok, TT * (head + 1))
                link(dve.reciprocal(stat[:, 2, head], stat[:, 1, head]))
                pr = prob[:, head % 2]
                dve.tensor_tensor(pr, pr, stat[:, 2, head].rearrange("p (t a) -> p t a", a=1).to_broadcast([P, TT, M]),
                                  ALU.mult).then_inc(pn_ok, 1)

            maxima(0)
            normalised(0)
            for head in range(XH):
                if head + 1 < XH:
                    maxima(head + 1)
                for m in range(MT):
                    dve.wait_ge(pth_ok, MT * head + m + 1)
                    low(pt_lo[:, head % 2, m], ps[m][:, :], pt_hi[:, head % 2, m]).then_inc(ptl_ok, 1)
                if head + 1 < XH:
                    normalised(head + 1)
                for n in range(HT):
                    o = head * HT + n
                    dve.wait_ge(mv_hi, S_O + o + 1)
                    low(a_lo[:, o], ps[2 + o % 2][:, :], a_hi[:, o]).then_inc(mv_lo, 1)
            dve.wait_ge(keyh_ok, 1)
            low(key_lo[:, :, :], key_raw[:, :, :], key_hi[:, :, :]).then_inc(keyl_ok, 1)

            residual(U_WO, KT)
            rsqrt_from(R_N3, 5, rms, T, D)
            dve.wait_ge(keyl_ok, 1)
            for k in range(KT):
                dve.scalar_tensor_tensor(q_raw[:, k], h[:, k], cst[:, C_GPEER + k:C_GPEER + k + 1], rms[:, :],
                                         ALU.mult, ALU.mult).then_inc(h_ok, 1)
                if k:
                    dve.wait_ge(mv_hi, S_N3 + k)
                    low(a_lo[:, k - 1], q_raw[:, k - 1], a_hi[:, k - 1]).then_inc(mv_lo, 1)
            dve.wait_ge(mv_hi, S_N3 + KT)
            low(a_lo[:, KT - 1], q_raw[:, KT - 1], a_hi[:, KT - 1]).then_inc(mv_lo, 1)

            with dve.Fori(0, KT // 4) as r:
                for k in range(4):
                    dve.wait_ge(qyh_ok, r * 4 + (k + 1))
                    low(qy_lo[:, k % 2], ps[k][:, :], qy_hi[:, k % 2]).then_inc(evac, 1)

            PER = 18
            dve.wait_ge(qs_ok, BANKS + KT)

            with dve.Fori(0, TT) as t:
                n = [0]

                def step(ins):
                    n[0] += 1
                    ins.then_inc(tk, 1)
                    dve.wait_ge(tk, t * PER + n[0])
                    dve.sem_inc(tk_seen, 1)

                def top16(vals, idx, src, rest, count):
                    for c in range(count):
                        last = dve.max(vals[:, c, 0:8], src[:, c])
                    step(last)
                    for c in range(count):
                        last = dve.match_replace(rest[:, c], vals[:, c, 0:8], src[:, c], LOWEST)
                    step(last)
                    for c in range(count):
                        last = dve.max(vals[:, c, 8:16], rest[:, c])
                    step(last)
                    for c in range(count):
                        dve.max_index(idx[:, c, 0:8], vals[:, c, 0:8], src[:, c])
                        last = dve.max_index(idx[:, c, 8:16], vals[:, c, 8:16], rest[:, c])
                    step(last)

                step(dve.tensor_copy(s_w[:, :, :], score[:, bass.ds(t, 1)].rearrange("p a h n -> p (a h) n")))
                top16(top_v, top_i, s_w, s_w2, HP)
                dve.tensor_copy(top_f[:, :, :], top_i[:, :, :])
                halves = top_v[:, :, :].rearrange("p (h s) k -> p h s k", s=2)
                for c in range(PH):
                    last = dve.tensor_tensor(cand[:, c].rearrange("p (a b) -> p a b", a=16),
                                             halves[:, c, 0].rearrange("p (a b) -> p a b", b=1).to_broadcast([P, 16, 16]),
                                             halves[:, c, 1:2].to_broadcast([P, 16, 16]), ALU.add)
                step(last)
                top16(best, pos, cand, cand2, PH)
                flat = pos[:, :, :].rearrange("p h k -> p (h k)")
                dve.tensor_scalar(pos_ab[:, 0], flat, 4, None, ALU.logical_shift_right)
                step(dve.tensor_scalar(pos_ab[:, 1], flat, 15, None, ALU.bitwise_and))
                dve.tensor_tensor(pick[:, 2, bass.ds(t, 1)].rearrange("p a (h k) -> p (a h) k", h=PH), best[:, :, :],
                                  best[:, :, 0:1].to_broadcast([P, PH, 16]), ALU.subtract)
                step(dve.tensor_copy(pos_f[:, :, :], pos_ab[:, :, :]))
                for s in range(2):
                    step(dve.tensor_tensor(match[:, :, :],
                                           pos_f[:, s].rearrange("p (n a) -> p n a", a=1).to_broadcast([P, HK, 16]),
                                           cst[:, C_IOTA:C_IOTA + 16].rearrange("p (a n) -> p a n", a=1).to_broadcast([P, HK, 16]),
                                           ALU.is_equal))
                    for c in range(PH):
                        m = match[:, c * TOPK:(c + 1) * TOPK, :]
                        last = dve.tensor_tensor(m, m, top_f[:, 2 * c + s:2 * c + s + 1, :].to_broadcast([P, TOPK, 16]), ALU.mult)
                    step(last)
                    step(dve.tensor_reduce(pick[:, s, bass.ds(t, 1)].rearrange("p a n -> p (a n)"), match[:, :, :],
                                           AX, ALU.add))
                assert n[0] == PER, n[0]
            dve.sem_inc(gexp_in, 1)
            dve.wait_ge(gexp_ok, 1)
            soft = pick[:, 2].rearrange("p t (h k) -> p (t h) k", k=TOPK)
            link(dve.tensor_reduce(gsum[:, 0], soft, AX, ALU.add))
            link(dve.reciprocal(gsum[:, 1], gsum[:, 0]))
            dve.tensor_tensor(soft, soft, gsum[:, 1].rearrange("p (n a) -> p n a", a=1).to_broadcast([P, TT * PH, TOPK]),
                              ALU.mult).then_inc(pick_ok, 1)
            dve.wait_ge(h_out, 16)
            dve.wait_ge(pick_ps, 1)
            dve.tensor_copy(i_T[:, :], ps[4][:, :]).then_inc(idx_ok, 1)
            dve.tensor_copy(j_T[:, :], ps[5][:, :]).then_inc(idx_ok, 1)
            dve.tensor_copy(gt_hi[:, :], ps[6][:, :]).then_inc(idx_ok, 1)
            dve.wait_ge(idx_ok, 3)
            low(gt_lo[:, :], ps[6][:, :], gt_hi[:, :]).then_inc(idx_ok, 1)
            dve.wait_ge(idx_ok, 4)
            def one_hots(b, n):
                slot = n % 2
                if not (isinstance(b, int) and b == 0 and n < 2):
                    dve.wait_ge(g_ps, b + (n - 1))
                for w in range(4):
                    tok = b * 4 + (4 * n + w)
                    col = slice(tok, tok + 1) if isinstance(b, int) else bass.ds(tok, 1)
                    dve.tensor_scalar(oh_i[:, 4 * slot + w], iota, i_T[:, col], None, ALU.is_equal)
                    dve.tensor_scalar(oh_jh[:, 4 * slot + w], iota, j_T[:, col], gt_hi[:, col].bitcast(F32),
                                      ALU.is_equal, ALU.mult)
                    last = dve.tensor_scalar(oh_jl[:, 4 * slot + w], iota, j_T[:, col], gt_lo[:, col].bitcast(F32),
                                             ALU.is_equal, ALU.mult)
                last.then_inc(oh_ok, 1)

            for n in range(2):
                one_hots(0, n)
            with dve.Fori(1, T // 8) as b:
                for n in range(2):
                    one_hots(b * 2, n)

            def gated(m, buf, n):
                s = n // 4
                if n % 4 == 0:
                    dve.wait_ge(ag_in[s], m * 32 + 32)
                a = ag[:, s, 0, n % 4]
                dve.tensor_tensor(a, a, ag[:, s, 1, n % 4], ALU.mult).then_inc(am_ok, 1)
                dve.wait_ge(ah_ok, m * EG + (n + 1))
                low(ga_lo[:, buf, n], a, ga_hi[:, buf, n]).then_inc(al_ok, 1)

            dve.wait_ge(unit_done, U_EV)
            dve.sem_inc(add_ok, BANKS)
            for n in range(EG):
                gated(0, 0, n)
            dve.wait_ge(h_back, 16)

            def v_group(g2, b, prep=True, squares=False):
                for c in range(DC):
                    if prep:
                        gated(g2 * 2 + (b + 1), 1 - b, c)
                    dve.wait_ge(unit_done, g2 * (2 * DC) + (U_EV + b * DC + c + 1))
                    for d in range(2):
                        k = 2 * c + d
                        dve.tensor_tensor(h[:, k], h[:, k], ps[k % 4][:, :], ALU.add).then_inc(add_ok, 1)
                    if squares:
                        for k in (2 * c, 2 * c + 1):
                            dve.wait_ge(add_ok, BANKS + KT * (NG - 1) + 2 * c + 2)
                            t = acc if k == 0 else sq
                            link(dve.tensor_tensor(t[:, :], h[:, k], h[:, k], ALU.mult))
                            if k:
                                link(dve.tensor_tensor(acc[:, :], acc[:, :], sq[:, :], ALU.add))

            with dve.Fori(0, NG // 2 - 1) as g2:
                v_group(g2, 0)
                v_group(g2, 1)
            v_group(NG // 2 - 1, 0)
            v_group(NG // 2 - 1, 1, prep=False, squares=True)
            dve.sem_inc(st_in, 1)
            rsqrt_from(R_FIN, 6, rms, T, D)
            for k in range(KT):
                dve.scalar_tensor_tensor(h[:, k], h[:, k], cst[:, C_GFIN + k:C_GFIN + k + 1], rms[:, :],
                                         ALU.mult, ALU.mult).then_inc(o_ok, 1)

        @block.tensor
        def _(pe):
            def three(out, wh, wl, mh, ml, start, stop):
                pe.matmul(out, wh, mh, start=start, stop=False)
                pe.matmul(out, wh, ml, start=False, stop=False)
                return pe.matmul(out, wl, mh, start=False, stop=stop)

            def unit(u, s, bank, hi, lo, cols, pidx, moving=None, order=range(KT), done=evac):
                pe.wait_ge(done, pidx + 1)
                for n, k in enumerate(order):
                    if n % 8 == 0:
                        pe.wait_ge(w_lo_ok, u * 2 + (k // 8 + 1))
                    if moving is not None:
                        pe.wait_ge(mv_lo, moving + n + 1)
                    w = slice(k * P, (k + 1) * P)
                    ins = three(ps[bank][:, 0:cols], w_hi[:, s, w], w_lo[:, s, w],
                                hi[:, k, 0:cols], lo[:, k, 0:cols], n == 0, n == KT - 1)
                ins.then_inc(unit_done, 1)

            def units(u0, n, hi, lo, cols, pidx, moving, order=range(KT)):
                with pe.Fori(0, n // 4) as r:
                    for k in range(4):
                        unit(r * 4 + (u0 + k), (u0 + k) % 2, k, hi, lo, cols, r * 4 + (pidx + k),
                             moving if k == 0 else None, order)

            def total(n, cols):
                pe.wait_ge(st_in, n + 1)
                pe.matmul(ps[7][:, 0:cols], ones, acc[:, 0:cols], start=True, stop=True).then_inc(st_ps, 1)

            pe.wait_ge(cst_in, 16)
            total(R_MEM, M)
            units(U_KV, KT, m_hi, m_lo, M, 0, S_MEM)
            def v_transpose(r, k):
                pe.wait_ge(kv_ok, r * 4 + (KT + k + 1))
                pe.wait_ge(kvl_ok, r * 4 + (KT - 4 + k + 1))
                for m in range(MT):
                    ins = pe.transpose(ps[4 + k][:, m * P:(m + 1) * P], kv_raw[:, k, m * P:(m + 1) * P], ident)
                ins.then_inc(vT_ok, 1)

            pe.wait_ge(st_ms, 1)
            with pe.Fori(0, XH) as r:
                for k in range(HT):
                    unit(r * 4 + (U_KV + KT + k), k % 2, k, m_hi, m_lo, M, r * 4 + (KT + k))
                    if k:
                        v_transpose(r, k - 1)
                v_transpose(r, HT - 1)
            pe.wait_ge(kvl_ok, 2 * KT)
            total(R_X, T)
            p0 = 2 * KT
            for i in range(NA):
                unit(U_IN + i, i % 2, i % 4, a_hi, a_lo, T, p0 + i, S_X if i == 0 else None)
            for i in range(NA):
                unit(U_IN + NA + i, i % 2, i % 4, a_hi, a_lo, T, p0 + NA + i)
                if i == 2:
                    total(R_LNMEAN, T)
                if i == NA - 1:
                    total(R_LNVAR, T)
            for i in range(NA):
                unit(U_IN + 2 * NA + i, i % 2, i % 4, a_hi, a_lo, T, p0 + 2 * NA + i)
                if i == 3:
                    pe.wait_ge(v_norm, NA)
                    for n in range(2 * TT):
                        t, c = n // 2, n % 2
                        if n >= 4:
                            pe.wait_ge(vtl_ok, n - 3)
                        for x in range(4):
                            ins = pe.transpose(ps[4 + n % 4][:, x * P:(x + 1) * P],
                                               v_fm[:, 4 * c + x, t * P:(t + 1) * P], ident)
                        ins.then_inc(vtt_ok, 1)
            pe.wait_ge(w_lo_ok, 2 * U_POOL + 2)
            pe.wait_ge(yl_ok, NA)
            pe.wait_ge(vtl_ok, 2 * TT)
            for o in range(NA):
                g = o // 2
                if o >= 4:
                    pe.wait_ge(mv_lo, S_POOL + o - 3)
                for c in range(2):
                    at_w = (g * 2 + c) * 256 + (o % 2) * P
                    s = U_POOL % 2
                    ins = three(ps[4 + o % 4][:, :], w_hi[:, s, at_w:at_w + P], w_lo[:, s, at_w:at_w + P],
                                y_hi[:, 2 * g + c], y_lo[:, 2 * g + c], c == 0, c == 1)
                ins.then_inc(pool_ps, 1)
            pe.wait_ge(pool_ps, NA)
            pe.sem_inc(unit_done, 1)
            pe.wait_ge(w_lo_ok, 2 * U_SGU + 2)
            s = U_SGU % 2
            for o in range(NA):
                pe.wait_ge(mv_lo, S_POOL + NA - 3 + o if o < 4 else S_SGU + o - 3)
                for b in range(TT):
                    f = slice(o * P, (o + 1) * P)
                    for seen, lo_i in ((64, 0), (128, 64)):
                        i = slice(o * P + lo_i, o * P + lo_i + 64)
                        ins = three(ps[4 + o % 4][:, b * P + lo_i:b * P + lo_i + 64], vt_hi[0:seen, b, f], vt_lo[0:seen, b, f],
                                    w_hi[0:seen, s, i], w_lo[0:seen, s, i], True, True)
                ins.then_inc(sgu_ps, 1)
            pe.wait_ge(sgu_ps, NA)
            pe.sem_inc(unit_done, 1)

            p0 += 3 * NA
            units(U_OUT, KT, a_hi, a_lo, T, p0, S_POOL, order=[*range(NA, KT), *range(NA)])
            p0 += KT

            def units_with_total(u0, p0, moving, n):
                for k in range(4):
                    unit(u0 + k, k % 2, k, a_hi, a_lo, T, p0 + k, moving if k == 0 else None)
                    if k == 1:
                        total(n, T)
                with pe.Fori(1, KT // 4) as r:
                    for k in range(4):
                        unit(r * 4 + (u0 + k), k % 2, k, a_hi, a_lo, T, r * 4 + (p0 + k))

            units_with_total(U_WQ, p0, S_N2, R_N2)
            p0 += KT

            def scores(head):
                s = head % 2
                pe.wait_ge(k_land[s], 16 * (head // 2 + 1))
                if head >= 2:
                    pe.wait_ge(ex_ok, TT * (head - 1))
                for t in range(TT):
                    for n in range(HT):
                        k = head * HT + n
                        if t == 0:
                            pe.wait_ge(mv_lo, S_Q + k + 1)
                        tok = slice(t * P, (t + 1) * P)
                        ins = three(ps[4 + 2 * s + t // 2][:, (t % 2) * M:(t % 2 + 1) * M], a_hi[:, k, tok], a_lo[:, k, tok],
                                    k_in[:, s, 0, n], k_in[:, s, 1, n], n == 0, n == HT - 1)
                ins.then_inc(sc_ps, 1)

            pe.wait_ge(evac, BANKS + p0)
            scores(0)
            scores(1)
            for head in range(XH):
                s = head % 2
                pe.wait_ge(pn_ok, head + 1)
                if head:
                    pe.wait_ge(ptl_ok, MT * head)
                for m in range(MT):
                    for t in range(TT):
                        ins = pe.transpose(ps[m][:, t * P:(t + 1) * P], prob[:, s, t, m * P:(m + 1) * P], ident)
                ins.then_inc(pT_ps, 1)
                pe.wait_ge(v_land[s], 16 * (head // 2 + 1))
                pe.wait_ge(ptl_ok, MT * (head + 1))
                for n in range(HT):
                    o = head * HT + n
                    if o >= 2:
                        pe.wait_ge(mv_lo, S_O + o - 1)
                    f = slice(n * P, (n + 1) * P)
                    for m in range(MT):
                        ins = three(ps[2 + o % 2][:, :], v_in[:, s, 0, m, f], v_in[:, s, 1, m, f],
                                    pt_hi[:, s, m], pt_lo[:, s, m], m == 0, m == MT - 1)
                    ins.then_inc(o_ps, 1)
                if head + 2 < XH:
                    scores(head + 2)
            pe.wait_ge(mv_lo, S_O + KT)
            units(U_WO, KT, a_hi, a_lo, T, p0, S_O)
            p0 += KT
            total(R_N3, T)
            pe.wait_ge(keyl_ok, 1)
            pe.wait_ge(st_ms, 5)
            pe.sem_inc(qs_ps, 3)

            def query_scores(r, k):
                pe.wait_ge(evac, r * 4 + (p0 + k + 1 + BANKS))
                pe.wait_ge(qs_ok, r * 4 + (k + 1))
                for t in range(TT):
                    tok = slice(t * P, (t + 1) * P)
                    kk = bass.ds(r * 4 + k, 1)
                    out = ps[4 + k][:, tok]
                    mh = key_hi[:, kk, :].rearrange("p a n -> p (a n)")
                    ml = key_lo[:, kk, :].rearrange("p a n -> p (a n)")
                    ins = three(out, qy_hi[:, k % 2, tok], qy_lo[:, k % 2, tok], mh, ml, True, True)
                ins.then_inc(qs_ps, 1)

            with pe.Fori(0, KT // 4) as r:
                for k in range(4):
                    unit(r * 4 + (U_QY + k), k % 2, k, a_hi, a_lo, T, r * 4 + (p0 + k), S_N3 if k == 0 else None)
                    if k:
                        query_scores(r, k - 1)
                query_scores(r, 3)

            p0 += KT
            pe.wait_ge(evac, BANKS + p0)

            def u_round(r):
                for k in range(4):
                    unit(r * 4 + (U_EU + k), k % 2, k, a_hi, a_lo, T, r * 4 + k, done=ea_ok)

            with pe.Fori(0, G_LEAD) as r:
                u_round(r)
            pe.wait_ge(qs_ok, BANKS + KT)
            pe.wait_ge(pick_ok, 1)
            for n in range(3):
                for t in range(TT):
                    ins = pe.transpose(ps[4 + n][:, t * P:(t + 1) * P], pick[:, n, t], ident)
            ins.then_inc(pick_ps, 1)
            pe.wait_ge(idx_ok, 4)

            def gates(b, n, first):
                pe.wait_ge(oh_ok, b + (n + 1))
                if not first:
                    pe.wait_ge(g_ok, b + (n - 3))
                for w in range(4):
                    x = 4 * (n % 2) + w
                    out = ps[4 + n % 4][:, w * P:(w + 1) * P]
                    pe.matmul(out, oh_jh[:, x], oh_i[:, x], start=True, stop=False)
                    ins = pe.matmul(out, oh_jl[:, x], oh_i[:, x], start=False, stop=True)
                ins.then_inc(g_ps, 1)

            def g_rounds(q):
                for part in range(4):
                    u_round(q * 4 + (G_LEAD + part))
                    for n in range(8):
                        gates(q * 32 + part * 8, n, isinstance(q, int) and q == 0 and part == 0 and n < 4)

            g_rounds(0)
            with pe.Fori(1, G_ROUNDS // 4) as q:
                g_rounds(q)
            with pe.Fori(G_LEAD + G_ROUNDS, ET // 4) as r:
                u_round(r)
            pe.wait_ge(ea_ok, BANKS + ET)

            def v_group(g2, b):
                for c in range(DC):
                    u = g2 * (2 * DC) + (U_EV + b * DC + c)
                    s = c % 2
                    pe.wait_ge(w_lo_ok, u * 2 + 2)
                    for d in range(2):
                        pe.wait_ge(add_ok, g2 * (2 * KT) + (b * KT + 2 * c + d + 1))
                        for n in range(EG):
                            if c == 0 and d == 0:
                                pe.wait_ge(al_ok, g2 * (2 * EG) + (b * EG + n + 1))
                            w = slice(n * 256 + d * P, n * 256 + (d + 1) * P)
                            ins = three(ps[(2 * c + d) % 4][:, :], w_hi[:, s, w], w_lo[:, s, w],
                                        ga_hi[:, b, n], ga_lo[:, b, n], n == 0, n == EG - 1)
                    ins.then_inc(unit_done, 1)

            with pe.Fori(0, NG // 2) as g2:
                v_group(g2, 0)
                v_group(g2, 1)
            total(R_FIN, T)


def _units(w):
    n = w.shape[1] // P
    return w.reshape(KT, P, n, P).transpose(2, 1, 0, 3).reshape(n, P, KT * P)


def _cols(v):
    return v.reshape(-1, P).T


def kernel(x, mem, g_mix, w_in, sgu_ln_g, sgu_ln_b, sgu_w, sgu_b, pool_w, pool_scale, w_out,
           g_xattn, g_mem, xattn_w_q, xattn_w_kv, xattn_w_o,
           g_peer, peer_w_query, peer_sub_keys, peer_u, peer_v, g_final):
    import numpy as np
    import concourse.bacc as bacc
    from concourse.bass_utils import run_bass_kernel_spmd

    def arr(a):
        return np.asarray(a)

    w = np.zeros((N_UNITS, P, 2048), np.float32)
    w[U_KV:U_IN] = _units(arr(xattn_w_kv)[0])
    win = _units(arr(w_in)[0])
    w[U_IN:U_IN + 2 * NA] = win[NA:]
    w[U_IN + 2 * NA:U_POOL] = win[:NA]
    w[U_POOL] = arr(pool_w)[0].reshape(4, 2, P, 256).transpose(2, 0, 1, 3).reshape(P, 2048)
    w[U_SGU, :, :NA * P] = arr(sgu_w)[0].transpose(2, 0, 1).reshape(P, NA * P)
    w[U_OUT:U_WQ] = _units(arr(w_out)[0])
    w[U_WQ:U_WO] = _units(arr(xattn_w_q)[0])
    w[U_WO:U_QY] = _units(arr(xattn_w_o)[0])
    w[U_QY:U_EU] = _units(arr(peer_w_query)[0])
    w[U_EU:U_EV] = arr(peer_u)[0].reshape(ET, P, KT, P).transpose(0, 3, 2, 1).reshape(ET, P, 2048)
    w[U_EV:] = arr(peer_v)[0].reshape(NG, EG, P, DC, 256).transpose(0, 3, 2, 1, 4).reshape(NG * DC, P, 2048)

    tokens = np.arange(16)
    counts = np.stack([1.0 / np.minimum(tokens + 1, w_) for w_ in (2, 4, 8, 16)]).astype(np.float32)
    const = np.concatenate([
        _cols(arr(g_mix)[0]), _cols(arr(g_xattn)[0]), _cols(arr(g_mem)[0]), _cols(arr(g_peer)[0]), _cols(arr(g_final)),
        _cols(arr(sgu_ln_g)[0]), _cols(arr(sgu_ln_b)[0]), _cols(arr(pool_scale)[0]),
        np.broadcast_to(counts.reshape(1, 64), (P, 64)), np.eye(P, dtype=np.float32), np.ones((P, P), np.float32),
        np.broadcast_to(np.arange(P, dtype=np.float32), (P, P)),
    ], axis=1)
    arrays = {
        "weights": w,
        "x_t": arr(x)[0].T.reshape(KT, P, T).transpose(1, 0, 2),
        "mem_t": arr(mem)[0].T.reshape(KT, P, M).transpose(1, 0, 2),
        "constants": const,
        "sgu_bias": np.broadcast_to(arr(sgu_b)[0][None], (P, NA, P)),
        "sub_keys": arr(peer_sub_keys)[0].reshape(HP, NK, P).transpose(2, 0, 1),
    }
    arrays = {name: np.ascontiguousarray(a) for name, a in arrays.items()}
    nc = bacc.Bacc("TRN2", target_bir_lowering=False, num_devices=1, dynamic_dma_scratch_size=1024)
    ins = [nc.dram_tensor(name, a.shape, F32, kind="ExternalInput").ap() for name, a in arrays.items()]
    out = nc.dram_tensor("out_t", (P, KT, T), F32, kind="ExternalOutput").ap()
    hybrid_block(nc, *ins, out)
    r = run_bass_kernel_spmd(nc, [arrays], core_ids=[0])
    return r.results[0]["out_t"].transpose(1, 0, 2).reshape(D, T).T.reshape(1, T, D).copy()
```

```python
from contextlib import ExitStack

import concourse.bass as bass
from concourse import mybir

F32 = mybir.dt.float32
F32R = mybir.dt.float32r
U32 = mybir.dt.uint32
ALU = mybir.AluOpType
ACT = mybir.ActivationFunctionType
AX = mybir.AxisListType.X

P = 128
D = 2048
KT = D // P
T = 512
TT = T // P
M = 256
MT = M // P
DA = 1024
NA = DA // P
XH = 4
HT = KT // XH
PH = 8
HP = 2 * PH
NK = 128
TOPK = 16
HK = PH * TOPK
NE = NK * NK
ET = NE // P
EG = 8
NG = ET // EG
DC = D // 256
EPS = 1e-6
SCALE = float(D // XH) ** -0.5
LOWEST = -3.4e38

U_KV = 0
U_IN = U_KV + 2 * KT
U_POOL = U_IN + 3 * NA
U_SGU = U_POOL + 1
U_OUT = U_SGU + 1
U_WQ = U_OUT + KT
U_WO = U_WQ + KT
U_QY = U_WO + KT
U_EU = U_QY + KT
U_EV = U_EU + ET
N_UNITS = U_EV + NG * DC

S_MEM, S_X, S_POOL, S_SGU, S_N2, S_Q, S_O, S_N3 = 0, 16, 32, 40, 48, 64, 80, 96
R_MEM, R_X, R_LNMEAN, R_LNVAR, R_N2, R_N3, R_FIN = range(7)
C_GMIX, C_GX, C_GMEM, C_GPEER, C_GFIN = 0, 16, 32, 48, 64
C_LNG, C_LNB, C_PSC, C_CNT, C_ID, C_ONE, C_IOTA = 80, 88, 96, 104, 168, 296, 424
N_CONST = 552

BANKS = 4
G_TOK = 64
G_LEAD = 9
U_LATE = 112
G_ROUNDS = T // G_TOK * 2


def hybrid_block(nc, wts, xT, memT, const, bs, keys, outT):
    kv_d = nc.dram_tensor("kv_split", (2 * XH, P, 2 * HT * M), F32).ap()
    h_d = nc.dram_tensor("h_spill", (P, KT, T), F32).ap()
    act_d = nc.dram_tensor("expert_act", (ET, P, T), F32).ap()
    g_d = nc.dram_tensor("gate_matrix", (T // G_TOK, P, NK, G_TOK), F32).ap()

    base = [(nc.sbuf_base + 127) // 128 * 128]

    def region(nbytes):
        at = base[0]
        base[0] += nbytes
        return at

    def at(name, shape, dt, offset):
        return nc.alloc_sbuf_tensor_at(name, shape, dt, offset=offset)

    KB = 1024
    r_w = region(48 * KB)
    w_raw = at("w_raw", [P, 2, 2048], F32, r_w)
    w_hi = at("w_hi", [P, 2, 2048], F32R, r_w + 16 * KB)
    w_lo = at("w_lo", [P, 2, 2048], F32R, r_w + 32 * KB)

    r_a = region(64 * KB)
    a_hi = at("a_hi", [P, KT, T], F32R, r_a)
    a_lo = at("a_lo", [P, KT, T], F32R, r_a + 32 * KB)
    x_sq = at("x_sq", [P, KT, T], F32, r_a)
    ga_hi = at("ga_hi", [P, 2, EG, T], F32R, r_a)
    ga_lo = at("ga_lo", [P, 2, EG, T], F32R, r_a + 32 * KB)

    r_h = region(32 * KB)
    h = at("h", [P, KT, T], F32, r_h)
    v_fm = at("v_fm", [P, NA, T], F32, r_h)
    pad = [at(f"pad{n}", [P, 16 + T], F32, r_h + 16 * KB + 2112 * n) for n in range(3)]
    y_raw = at("y_raw", [P, 3, T], F32, r_h + 16 * KB + 6336)
    ln_st = at("ln_st", [P, T], F32, r_h + 16 * KB + 12480)
    vt_lo = at("vt_lo", [P, TT, DA], F32R, r_h + 16 * KB)
    e_act = at("e_act", [P, 4, T], F32, r_h)
    i_T = at("i_T", [P, T], F32, r_h + 8 * KB)
    j_T = at("j_T", [P, T], F32, r_h + 10 * KB)
    gt_hi = at("gt_hi", [P, T], F32R, r_h + 12 * KB)
    gt_lo = at("gt_lo", [P, T], F32R, r_h + 14 * KB)
    oh_j = at("oh_j", [P, 8, P], F32R, r_h + 16 * KB)
    oh_i = at("oh_i", [P, 8, 2, P], F32R, r_h + 20 * KB)

    r_q = region(32 * KB)
    mem_raw = at("mem_raw", [P, KT, M], F32, r_q)
    mem_sq = at("mem_sq", [P, KT, M], F32, r_q + 16 * KB)
    kv_out = at("kv_out", [P, XH, 2, HT * M], F32R, r_q)
    vt_hi = at("vt_hi", [P, TT, DA], F32R, r_q)
    u_act = at("u_act", [P, NA, T], F32, r_q + 16 * KB)
    q_raw = at("q_raw", [P, KT, T], F32, r_q)
    prob = at("prob", [P, 2, TT, M], F32, r_q)
    pt_hi = at("pt_hi", [P, 2, MT, T], F32R, r_q + 8 * KB)
    pt_lo = at("pt_lo", [P, 2, MT, T], F32R, r_q + 16 * KB)
    key_raw = at("key_raw", [P, HP, NK], F32, r_q)
    score = at("score", [P, TT, HP, NK], F32, r_q)
    a_in = at("a_in", [P, 2, 4, T], F32, r_q)
    g_in = at("g_in", [P, 2, T // G_TOK, 4, G_TOK], F32, r_q + 16 * KB)

    r_k = region(32 * KB)
    m_hi = at("m_hi", [P, KT, M], F32R, r_k)
    m_lo = at("m_lo", [P, KT, M], F32R, r_k + 16 * KB)
    y_hi = at("y_hi", [P, NA, T], F32R, r_k)
    y_lo = at("y_lo", [P, NA, T], F32R, r_k + 16 * KB)
    k_in = at("k_in", [P, 2, 2, HT, M], F32R, r_k)
    v_in = at("v_in", [P, 2, 2, MT, 512], F32R, r_k + 16 * KB)
    key_hi = at("key_hi", [P, HP, NK], F32R, r_k)
    key_lo = at("key_lo", [P, HP, NK], F32R, r_k + 8 * KB)
    qy_hi = at("qy_hi", [P, 2, T], F32R, r_k + 16 * KB)
    qy_lo = at("qy_lo", [P, 2, T], F32R, r_k + 20 * KB)
    s_w = at("s_w", [P, HP, NK], F32, r_k)
    s_w2 = at("s_w2", [P, HP, NK], F32, r_k + 8 * KB)
    cand = at("cand", [P, PH, 256], F32, r_k + 16 * KB)
    cand2 = at("cand2", [P, PH, 256], F32, r_k)
    match = at("match", [P, HK, 16], F32, r_k + 8 * KB)
    top_v = at("top_v", [P, HP, 16], F32, r_k + 24 * KB)
    top_i = at("top_i", [P, HP, 16], U32, r_k + 25 * KB)
    top_f = at("top_f", [P, HP, 16], F32, r_k + 26 * KB)
    best = at("best", [P, PH, 16], F32, r_k + 27 * KB)
    pos = at("pos", [P, PH, 16], U32, r_k + 27 * KB + 512)
    pos_ab = at("pos_ab", [P, 2, HK], U32, r_k + 28 * KB)
    pos_f = at("pos_f", [P, 2, HK], F32, r_k + 29 * KB)
    g_out = at("g_out", [P, 2, NK, G_TOK], F32, r_q)

    rms = at("rms", [P, T], F32, region(2 * KB))
    acc = at("acc", [P, T], F32, region(2 * KB))
    sq = at("sq", [P, T], F32, region(2 * KB))
    r_s = region(6 * KB)
    kv_raw = at("kv_raw", [P, 4, M], F32, r_s)
    bias_s = at("bias_s", [P, NA, P], F32, r_s)
    stat = at("stat", [P, 3, XH, TT], F32, r_s)
    pick = at("pick", [P, 3, TT, HK], F32, r_s)
    gsum = at("gsum", [P, 2, TT * PH], F32, region(256))
    cst = at("cst", [P, N_CONST], F32, region(4 * N_CONST))
    assert base[0] <= nc.sbuf_usable_end, base[0]

    ident = cst[:, C_ID:C_ID + P]
    ones = cst[:, C_ONE:C_ONE + P]
    iota = cst[:, C_IOTA:C_IOTA + P]

    ctx = ExitStack()
    with ctx:
        ps = [ctx.enter_context(nc.psum_tensor(f"ps{n}", [P, 512], F32)) for n in range(8)]

        def sem(name):
            return ctx.enter_context(nc.semaphore(name))

        w_landed = [sem("w_landed0"), sem("w_landed1")]
        w_hi_ok, w_lo_ok = sem("w_hi_ok"), sem("w_lo_ok")
        unit_done = sem("unit_done")
        evac = sem("evac")
        mv_hi, mv_lo = sem("mv_hi"), sem("mv_lo")
        mem_in = [sem(f"mem_in{n}") for n in range(4)]
        x_in, x_back, cst_in, bias_in, key_in = (
            sem("x_in"), sem("x_back"), sem("cst_in"), sem("bias_in"), sem("key_in"))
        xs_ok = sem("xs_ok")
        sq_ok = sem("sq_ok")
        st_in, st_ps, st_ms, st_rt = sem("st_in"), sem("st_ps"), sem("st_ms"), sem("st_rt")
        chain = sem("chain")
        kv_ok, kvh_ok, kvl_ok = sem("kv_ok"), sem("kvh_ok"), sem("kvl_ok")
        kv_store = sem("kv_store")
        vT_ok = sem("vT_ok")
        v_ok, v_gelu, v_norm = sem("v_ok"), sem("v_gelu"), sem("v_norm")
        y_ok, yh_ok, yl_ok = sem("y_ok"), sem("yh_ok"), sem("yl_ok")
        vtt_ok, vth_ok, vtl_ok = sem("vtt_ok"), sem("vth_ok"), sem("vtl_ok")
        u_ok, u_gelu = sem("u_ok"), sem("u_gelu")
        pool_ps, sgu_ps, sgu_y = sem("pool_ps"), sem("sgu_ps"), sem("sgu_y")
        sgu_masked = sem("sgu_masked")
        h_ok, hs_ok, acc_ok = sem("h_ok"), sem("hs_ok"), sem("acc_ok")
        q_ok = sem("q_ok")
        k_land = [sem("k_land0"), sem("k_land1")]
        v_land = [sem("v_land0"), sem("v_land1")]
        sc_ps, mx_ok, ex_ok, pn_ok = sem("sc_ps"), sem("mx_ok"), sem("ex_ok"), sem("pn_ok")
        pT_ps, pth_ok, ptl_ok, o_ps = sem("pT_ps"), sem("pth_ok"), sem("ptl_ok"), sem("o_ps")
        keyh_ok, keyl_ok = sem("keyh_ok"), sem("keyl_ok")
        qyh_ok, qs_ps, qs_ok = sem("qyh_ok"), sem("qs_ps"), sem("qs_ok")
        h_out, h_back = sem("h_out"), sem("h_back")
        ea_ok = sem("ea_ok")
        ea_out = [sem(f"ea_out{n}") for n in range(4)]
        tk = sem("tk")
        tk_seen = sem("tk_seen")
        gexp_in, gexp_ok = sem("gexp_in"), sem("gexp_ok")
        pick_ok, pick_ps, idx_ok = sem("pick_ok"), sem("pick_ps"), sem("idx_ok")
        oh_ok, g_ps, g_ok = sem("oh_ok"), sem("g_ps"), sem("g_ok")
        g_st = [sem("g_st0"), sem("g_st1")]
        n3_half = sem("n3_half")
        ag_in = [sem("ag_in0"), sem("ag_in1")]
        am_ok, ah_ok, al_ok = sem("am_ok"), sem("ah_ok"), sem("al_ok")
        add_ok = sem("add_ok")
        o_ok, o_st = sem("o_ok"), sem("o_st")

        block = ctx.enter_context(nc.Block())

        @block.sync
        def _(sp):
            def load_unit(u, slot, first=False):
                if not first:
                    sp.wait_ge(w_lo_ok, u * 2 - 2)
                src = wts[u] if isinstance(u, int) else wts[bass.ds(u, 1)].rearrange("a p n -> (a p) n")
                sp.dma_start(w_raw[:, slot], src).then_inc(w_landed[slot], 16)

            def load_units(u0, n):
                with sp.Fori(0, n // 2) as i:
                    load_unit(i * 2 + u0, 0)
                    load_unit(i * 2 + (u0 + 1), 1)

            load_unit(0, 0, True)
            sp.dma_start(cst[:, :], const).then_inc(cst_in, 16)
            for c in range(4):
                m4 = slice(4 * c, 4 * c + 4)
                sp.dma_start(mem_raw[:, m4], memT[:, m4]).then_inc(mem_in[c], 16)
            load_unit(1, 1, True)
            for c in range(4):
                load_unit(2 + c, c % 2)
                x4 = slice(4 * c, 4 * c + 4)
                sp.dma_start(h[:, x4], xT[:, x4]).then_inc(x_in, 16)
            load_units(6, U_IN - 6)
            load_units(U_IN, 4)
            sp.wait_ge(kvl_ok, 2 * KT)
            sp.dma_start(bias_s[:, :, :], bs).then_inc(bias_in, 16)
            load_units(U_IN + 4, U_OUT - U_IN - 4)
            load_units(U_OUT, 2)
            sp.wait_ge(sgu_ps, NA)
            sp.dma_start(h[:, :, :], xT).then_inc(x_back, 16)
            load_units(U_OUT + 2, KT - 2)

            def load_kv(head):
                s = head % 2
                if head == 0:
                    sp.wait_ge(pool_ps, NA)
                    sp.wait_ge(kv_store, 16 * 2 * XH)
                if head >= 2:
                    sp.wait_ge(sc_ps, head - 1)
                sp.dma_start(k_in[:, s].rearrange("p a t m -> p (a t m)").bitcast(F32), kv_d[head]).then_inc(k_land[s], 16)
                if head >= 2:
                    sp.wait_ge(o_ps, HT * (head - 1))
                sp.dma_start(v_in[:, s].rearrange("p a t m -> p (a t m)").bitcast(F32), kv_d[XH + head]).then_inc(v_land[s], 16)

            load_kv(0)
            load_kv(1)
            load_units(U_WQ, KT + 2)
            load_kv(2)
            load_kv(3)
            sp.wait_ge(o_ps, XH * HT)
            sp.dma_start(key_raw[:, :, :], keys).then_inc(key_in, 16)
            load_units(U_WO + 2, 2 * KT - 2)
            load_units(U_EU, U_LATE)

            def load_ag(m, first=False, halves=range(2)):
                for s in halves:
                    mm = m * 2 + s
                    if not first:
                        sp.wait_ge(al_ok, mm * 4 - 4)
                    tiles = slice(mm * 4, mm * 4 + 4) if isinstance(mm, int) else bass.ds(mm * 4, 4)
                    sp.dma_start(a_in[:, s], act_d[tiles].rearrange("e p t -> p e t")).then_inc(ag_in[s], 16)
                    sp.dma_start(g_in[:, s].rearrange("p b e t -> p b (e t)"),
                                 g_d[:, :, tiles].rearrange("b p e t -> p b (e t)")).then_inc(ag_in[s], 16)

            for s in range(2):
                sp.wait_ge(g_st[s], 16 * (T // G_TOK // 2))
            for s in range(4):
                sp.wait_ge(ea_out[s], 16 * (EG // 4))
            load_ag(0, True)
            sp.wait_ge(h_out, 16)
            sp.wait_ge(g_ps, T // 4)
            sp.dma_start(h[:, 4:KT], h_d[:, 4:KT]).then_inc(h_back, 16)
            load_units(U_EU + U_LATE, ET - U_LATE + 2)
            load_unit(U_EV + 2, 0)
            load_ag(1, halves=[0])
            for s in range(4):
                sp.wait_ge(ea_out[s], 16 * (ET // 4))
            sp.dma_start(h[:, 0:4], h_d[:, 0:4]).then_inc(h_back, 16)
            load_ag(1, halves=[1])
            for u in range(U_EV + 3, U_EV + DC + 2):
                load_unit(u, u % 2)
            with sp.Fori(1, NG - 1) as g:
                for c in range(0, DC, 2):
                    load_unit(g * DC + (U_EV + 2 + c), 0)
                    load_unit(g * DC + (U_EV + 3 + c), 1)
                    if c == 0:
                        load_ag(g + 1)
            for u in range(N_UNITS - DC + 2, N_UNITS):
                load_unit(u, u % 2)
            for k in range(0, KT, 4):
                sp.wait_ge(o_ok, k + 4)
                sp.dma_start(outT[:, k:k + 4], h[:, k:k + 4]).then_inc(o_st, 16)
            sp.wait_ge(o_st, 16 * (KT // 4))

        @block.gpsimd
        def _(pool):
            with pool.Fori(0, N_UNITS // 2) as i:
                for s in range(2):
                    for half in range(2):
                        pool.wait_ge(w_hi_ok, i * 4 + (2 * s + half + 1))
                        c = slice(half * 1024, half * 1024 + 1024)
                        pool.tensor_tensor(w_lo[:, s, c], w_raw[:, s, c], w_hi[:, s, c].bitcast(F32),
                                           ALU.subtract).then_inc(w_lo_ok, 1)

        @block.scalar
        def _(act):
            def w_high(i, c, first=False):
                s = c % 2
                act.wait_ge(w_landed[s], i * 16 + (c // 2 * 16 + 16))
                if not first:
                    act.wait_ge(unit_done, i * 2 + (c - 1))
                for half in range(2):
                    cc = slice(half * 1024, half * 1024 + 1024)
                    act.activation(w_hi[:, s, cc], w_raw[:, s, cc], ACT.Copy).then_inc(w_hi_ok, 1)

            def units(u0, n):
                assert u0 % 2 == 0 and n % 2 == 0
                with act.Fori(0, (n - 2) // 2) as r:
                    for k in range(2):
                        w_high(r, u0 + 2 + k)
                w_high(0, u0 + n)

            def resume(u0):
                w_high(0, u0 + 1)

            def sqrt_of(count, t, cols):
                act.wait_ge(st_ms, count)
                act.activation(t[:, 0:cols], t[:, 0:cols], ACT.Sqrt).then_inc(st_rt, 1)

            w_high(0, 0, True)
            act.wait_ge(cst_in, 16)
            for k in range(KT):
                if k % 4 == 0:
                    act.wait_ge(mem_in[k // 4], 16)
                act.activation(m_hi[:, k], mem_raw[:, k], ACT.Copy,
                               scale=cst[:, C_GMEM + k:C_GMEM + k + 1]).then_inc(mv_hi, 1)
            w_high(0, 1, True)
            act.activation(mem_sq[:, :, :], mem_raw[:, :, :], ACT.Square).then_inc(sq_ok, 1)
            w_high(0, 2)
            w_high(0, 3)
            sqrt_of(1, rms, M)

            def k_round(r, first=False):
                for k in range(HT):
                    if not (first and k < 2):
                        w_high(r * 2, U_KV + 2 + k)
                    act.wait_ge(kv_ok, r * HT + (k + 1))
                    if k == 0:
                        act.wait_ge(mv_lo, KT)
                    act.activation(kv_out[:, bass.ds(r, 1), 0, k * M:(k + 1) * M], kv_raw[:, k:k + 1],
                                   ACT.Copy).then_inc(kvh_ok, 1)
                    if k == 2:
                        act.wait_ge(x_in, r * 16 + 16)
                        act.activation(x_sq[:, bass.ds(r * 4, 4), :], h[:, bass.ds(r * 4, 4), :],
                                       ACT.Square).then_inc(sq_ok, 1)
                act.wait_ge(kvl_ok, r * HT + HT)
                act.dma_start(kv_d[bass.ds(r, 1)].rearrange("a p n -> p (a n)"),
                              kv_out[:, bass.ds(r, 1)].rearrange("p a s n -> p (a s n)").bitcast(F32)).then_inc(kv_store, 16)

            k_round(0, True)
            with act.Fori(1, XH) as r:
                k_round(r)
            w_high(0, U_KV + KT + 2)

            def x_high(r, k):
                act.wait_ge(st_in, R_X + 1)
                kk = bass.ds(r * 4 + k, 1)
                act.activation(a_hi[:, kk, :], h[:, kk, :], ACT.Copy,
                               scale=cst[:, bass.ds(r * 4 + (C_GMIX + k), 1)]).then_inc(mv_hi, 1)

            def v_high(r, k):
                act.wait_ge(kv_store, 16 * XH)
                act.wait_ge(vT_ok, r * HT + (k + 1))
                act.activation(kv_out[:, bass.ds(r, 1), 0].rearrange("p a (t n) -> p (a t) n", t=MT)[:, :, k * P:(k + 1) * P],
                               ps[4 + k][:, 0:M].rearrange("p (t n) -> p t n", t=MT), ACT.Copy).then_inc(kvh_ok, 1)

            with act.Fori(0, XH) as r:
                for k in range(HT):
                    if k:
                        w_high(r * 2, U_KV + KT + 2 + k)
                        v_high(r, k - 1)
                    x_high(r, k)
                v_high(r, HT - 1)
                act.wait_ge(kvl_ok, r * HT + (KT + HT))
                act.dma_start(kv_d[bass.ds(r + XH, 1)].rearrange("a p n -> p (a n)"),
                              kv_out[:, bass.ds(r, 1)].rearrange("p a s n -> p (a s n)").bitcast(F32)).then_inc(kv_store, 16)
                w_high(r * 2, U_KV + KT + 2 + HT)
            sqrt_of(2, rms, T)
            w_high(0, U_IN + 3)
            act.wait_ge(kv_store, 16 * 2 * XH)

            for i in range(NA):
                act.wait_ge(v_ok, i + 1)
                act.activation(v_fm[:, i], v_fm[:, i], ACT.Gelu).then_inc(v_gelu, 1)
                if i < NA - 1:
                    w_high(0, U_IN + 4 + i)
            for i in range(NA):
                w_high(0, U_IN + NA + 3 + i)
                act.wait_ge(y_ok, i + 1)
                act.activation(y_hi[:, i], y_raw[:, i % 3], ACT.Copy).then_inc(yh_ok, 1)
            sqrt_of(3, ln_st, T)
            for i in range(NA):
                act.wait_ge(u_ok, i + 1)
                act.activation(u_act[:, i], u_act[:, i], ACT.Gelu).then_inc(u_gelu, 1)
                if i == 3:
                    for n in range(2 * TT):
                        act.wait_ge(vtt_ok, n + 1)
                        t, c = n // 2, n % 2
                        act.activation(vt_hi[:, t, c * 512:c * 512 + 512], ps[4 + n % 4][:, :],
                                       ACT.Copy).then_inc(vth_ok, 1)
                if i == NA - 2:
                    act.wait_ge(sgu_masked, 1)
                if i < NA - 1:
                    w_high(0, U_IN + 2 * NA + 3 + i)
            for o in range(NA):
                act.wait_ge(pool_ps, o + 1)
                if o == 0:
                    act.wait_ge(unit_done, U_POOL)
                act.activation(a_hi[:, NA + o], ps[4 + o % 4][:, :], ACT.Copy,
                               scale=cst[:, C_PSC + o:C_PSC + o + 1]).then_inc(mv_hi, 1)
            w_high(0, U_OUT)
            for o in range(NA):
                act.wait_ge(sgu_y, o + 1)
                act.activation(a_hi[:, o], u_act[:, o], ACT.Copy).then_inc(mv_hi, 1)
            w_high(0, U_OUT + 1)

            def scaled_high(gain, end):
                act.wait_ge(unit_done, end)
                for k in range(KT):
                    act.activation(a_hi[:, k], h[:, k], ACT.Copy,
                                   scale=cst[:, gain + k:gain + k + 1]).then_inc(mv_hi, 1)
                    if k == 7:
                        resume(end)

            units(U_OUT, KT)
            act.wait_ge(h_ok, KT)
            scaled_high(C_GX, U_WQ)
            sqrt_of(4, rms, T)
            units(U_WQ, KT)

            act.wait_ge(unit_done, U_WO)
            for k in range(KT):
                act.wait_ge(q_ok, k + 1)
                act.activation(a_hi[:, k], q_raw[:, k], ACT.Copy).then_inc(mv_hi, 1)
            act.wait_ge(mv_lo, S_Q + KT)

            def exps(head, tiles=range(TT)):
                act.wait_ge(mx_ok, head + 1)
                if head >= 2:
                    act.wait_ge(pT_ps, head - 1)
                for t in tiles:
                    act.activation(prob[:, head % 2, t],
                                   ps[4 + 2 * (head % 2) + t // 2][:, (t % 2) * M:(t % 2 + 1) * M], ACT.Exp,
                                   bias=stat[:, 0, head, t:t + 1], scale=SCALE,
                                   accum_out=stat[:, 1, head, t:t + 1]).then_inc(ex_ok, 1)

            exps(0)
            for head in range(XH):
                act.wait_ge(pT_ps, head + 1)
                if head >= 2:
                    act.wait_ge(o_ps, HT * (head - 1))
                for m in range(MT):
                    act.activation(pt_hi[:, head % 2, m], ps[m][:, :], ACT.Copy).then_inc(pth_ok, 1)
                for n in range(HT):
                    o = head * HT + n
                    act.wait_ge(o_ps, o + 1)
                    act.activation(a_hi[:, o], ps[2 + o % 2][:, :], ACT.Copy).then_inc(mv_hi, 1)
                    if head + 1 < XH and n < 2:
                        exps(head + 1, range(n * 2, n * 2 + 2))
            resume(U_WO)
            act.wait_ge(key_in, 16)
            act.activation(key_hi[:, :, :], key_raw[:, :, :], ACT.Copy).then_inc(keyh_ok, 1)

            units(U_WO, KT)
            sqrt_of(5, rms, T)
            for k in range(KT):
                act.wait_ge(h_ok, 2 * KT + k + 1)
                act.activation(a_hi[:, k], q_raw[:, k], ACT.Copy).then_inc(mv_hi, 1)
                if k == 7:
                    resume(U_QY)
            act.dma_start(h_d, h[:, :, :]).then_inc(h_out, 16)

            act.sem_inc(qs_ok, BANKS)
            act.wait_ge(mv_lo, S_N3 + KT)

            def query_high(r, k):
                act.wait_ge(unit_done, r * 4 + (U_QY + k + 1))
                act.wait_ge(qs_ps, r * 4 + (k + 2))
                act.activation(qy_hi[:, k % 2], ps[k][:, :], ACT.Copy).then_inc(qyh_ok, 1)

            def score_copy(r, k):
                act.wait_ge(qs_ps, r * 4 + (k + 4))
                act.activation(score[:, :, bass.ds(r * 4 + k, 1), :],
                               ps[4 + k % 4][:, :].rearrange("p (t a n) -> p t a n", t=TT, a=1),
                               ACT.Copy).then_inc(qs_ok, 1)

            def query_round(r, first=False):
                for k in range(4):
                    w_high(r * 2, U_QY + 2 + k)
                    query_high(r, k)
                    if not (first and k == 0):
                        score_copy(r, k - 1)

            query_round(0, True)
            with act.Fori(1, KT // 4) as r:
                query_round(r)
            act.sem_inc(ea_ok, BANKS)
            score_copy(KT // 4, -1)

            act.wait_ge(h_out, 16)

            def u_round(r, before_last=None):
                for k in range(4):
                    if k == 3 and before_last is not None:
                        before_last()
                    w_high(r * 2, U_EU + 2 + k)
                    act.wait_ge(unit_done, r * 4 + (U_EU + k + 1))
                    if not (isinstance(r, int) and r == 0):
                        act.wait_ge(ea_out[k], r * 16)
                    act.activation(e_act[:, k], ps[k][:, :], ACT.Gelu).then_inc(ea_ok, 1)
                    act.wait_ge(ea_ok, r * 4 + (BANKS + k + 1))
                    dst = act_d[r * 4 + k] if isinstance(r, int) else act_d[bass.ds(r * 4 + k, 1)].rearrange("a p t -> (a p) t")
                    act.dma_start(dst, e_act[:, k]).then_inc(ea_out[k], 16)

            u_round(0)
            with act.Fori(1, G_LEAD - 1) as r:
                u_round(r)
            act.wait_ge(gexp_in, 1)
            act.activation(pick[:, 2], pick[:, 2], ACT.Exp).then_inc(gexp_ok, 1)
            u_round(G_LEAD - 1)

            def g_rounds(q):
                for slot in range(2):
                    for x in range(2):
                        u_round(q * 4 + (G_LEAD + 2 * slot + x))
                    act.wait_ge(g_ok, q * 32 + (slot * 16 + 16))
                    dst = g_d[q * 2 + slot] if isinstance(q, int) else g_d[bass.ds(q * 2 + slot, 1)].rearrange("a p i t -> (a p) i t")
                    act.dma_start(dst, g_out[:, slot]).then_inc(g_st[slot], 16)

            g_rounds(0)
            with act.Fori(1, G_ROUNDS // 4) as q:
                g_rounds(q)
            with act.Fori(G_LEAD + G_ROUNDS, ET // 4 - 1) as r:
                u_round(r)

            def gated_high(m, buf, n):
                act.wait_ge(am_ok, m * EG + (n + 1))
                act.activation(ga_hi[:, buf, n], a_in[:, n // 4, n % 4], ACT.Copy).then_inc(ah_ok, 1)

            def first_gated():
                act.wait_ge(n3_half, 1)
                for n in range(EG):
                    gated_high(0, 0, n)

            u_round(ET // 4 - 1, first_gated)

            def v_group(g2, b, prep=True, ends=False):
                for c in range(DC):
                    u = U_EV + b * DC + c + 2
                    if not (ends and c >= DC - 2):
                        w_high(g2 * DC, u)
                    if prep:
                        gated_high(g2 * 2 + (b + 1), 1 - b, c)

            with act.Fori(0, NG // 2 - 1) as g2:
                v_group(g2, 0)
                v_group(g2, 1)
            v_group(NG // 2 - 1, 0)
            v_group(NG // 2 - 1, 1, prep=False, ends=True)
            sqrt_of(6, rms, T)

        @block.vector
        def _(dve):
            steps = [0]

            def link(ins):
                steps[0] += 1
                ins.then_inc(chain, 1)
                dve.wait_ge(chain, steps[0])

            def low(out, src, hi, gain=None):
                if gain is None:
                    ins = dve.tensor_tensor(out, src, hi.bitcast(F32), ALU.subtract)
                else:
                    ins = dve.scalar_tensor_tensor(out, src, cst[:, gain:gain + 1], hi.bitcast(F32),
                                                   ALU.mult, ALU.subtract)
                return ins

            def mean_from(n, t, cols, width, eps):
                dve.wait_ge(st_ps, n + 1)
                return dve.tensor_scalar(t[:, 0:cols], ps[7][:, 0:cols], 1.0 / width, eps, ALU.mult, ALU.add)

            def rsqrt_from(n, count, t, cols, width):
                mean_from(n, t, cols, width, EPS).then_inc(st_ms, 1)
                dve.wait_ge(st_rt, count)
                link(dve.reciprocal(t[:, 0:cols], t[:, 0:cols]))

            def evacuated(u):
                dve.wait_ge(unit_done, u + 1)

            dve.sem_inc(evac, BANKS)
            dve.wait_ge(cst_in, 16)
            for k in range(KT):
                dve.wait_ge(mv_hi, S_MEM + k + 1)
                low(m_lo[:, k], mem_raw[:, k], m_hi[:, k], C_GMEM + k).then_inc(mv_lo, 1)
            dve.wait_ge(sq_ok, 1)
            dve.tensor_reduce(acc[:, 0:M], mem_sq[:, :, :].rearrange("p k t -> p t k"), AX, ALU.add).then_inc(st_in, 1)
            rsqrt_from(R_MEM, 1, rms, M, D)
            link(dve.memset(acc[:, :], 0.0))
            def kv_scale(r, k, u0, n0):
                evacuated(r * 4 + (u0 + k))
                dve.tensor_tensor(kv_raw[:, k], ps[k][:, 0:M], rms[:, 0:M], ALU.mult).then_inc(kv_ok, 1)
                dve.wait_ge(kv_ok, r * 4 + (n0 + k + 1))
                dve.sem_inc(evac, 1)

            with dve.Fori(0, XH) as r:
                for k in range(HT):
                    kv_scale(r, k, U_KV, 0)
                    dve.wait_ge(kvh_ok, r * 4 + (k + 1))
                    low(kv_out[:, bass.ds(r, 1), 1, k * M:(k + 1) * M], kv_raw[:, k:k + 1],
                        kv_out[:, bass.ds(r, 1), 0, k * M:(k + 1) * M]).then_inc(kvl_ok, 1)
                dve.wait_ge(sq_ok, r + 2)
                dve.tensor_reduce(sq[:, :], x_sq[:, bass.ds(r * 4, 4), :].rearrange("p k t -> p t k"),
                                  AX, ALU.add).then_inc(xs_ok, 1)
                dve.wait_ge(xs_ok, r * 2 + 1)
                dve.tensor_tensor(acc[:, :], acc[:, :], sq[:, :], ALU.add).then_inc(xs_ok, 1)
            dve.wait_ge(xs_ok, 2 * XH)
            dve.sem_inc(st_in, 1)
            def v_low(r, k):
                dve.wait_ge(kvh_ok, r * 4 + (KT + k + 1))
                low(kv_out[:, bass.ds(r, 1), 1].rearrange("p a (t n) -> p (a t) n", t=MT)[:, :, k * P:(k + 1) * P],
                    ps[4 + k][:, 0:M].rearrange("p (t n) -> p t n", t=MT),
                    kv_out[:, bass.ds(r, 1), 0].rearrange("p a (t n) -> p (a t) n", t=MT)[:, :, k * P:(k + 1) * P]
                    ).then_inc(kvl_ok, 1)

            with dve.Fori(0, XH) as r:
                for k in range(HT):
                    kv_scale(r, k, U_KV + KT, KT)
                    if k:
                        v_low(r, k - 1)
                    dve.wait_ge(mv_hi, r * 4 + (S_X + k + 1))
                    kk = bass.ds(r * 4 + k, 1)
                    dve.scalar_tensor_tensor(a_lo[:, kk, :], h[:, kk, :], cst[:, bass.ds(r * 4 + (C_GMIX + k), 1)],
                                             a_hi[:, kk, :].bitcast(F32), ALU.mult, ALU.subtract).then_inc(mv_lo, 1)
                v_low(r, HT - 1)

            rsqrt_from(R_X, 2, rms, T, D)
            for i in range(NA):
                evacuated(U_IN + i)
                dve.tensor_tensor(v_fm[:, i], ps[i % 4][:, :], rms[:, :], ALU.mult).then_inc(v_ok, 1)
                dve.wait_ge(v_ok, i + 1)
                dve.sem_inc(evac, 1)
                dve.wait_ge(v_gelu, i + 1)
                if i == 1:
                    link(dve.tensor_tensor(acc[:, :], v_fm[:, 0], v_fm[:, 1], ALU.add))
                elif i > 1:
                    link(dve.tensor_tensor(acc[:, :], acc[:, :], v_fm[:, i], ALU.add))
            dve.sem_inc(st_in, 1)
            for t in pad:
                link(dve.memset(t[:, 0:16], 0.0))

            def pooled(i):
                w = 2 << (i // 2)
                evacuated(U_IN + NA + i)
                x = pad[0]
                link(dve.tensor_tensor(x[:, 16:16 + T], ps[i % 4][:, :], rms[:, :], ALU.mult))
                dve.sem_inc(evac, 1)
                src, n, s = x, 1, 1
                while s < w:
                    dst = pad[n]
                    link(dve.tensor_tensor(dst[:, 16:16 + T], src[:, 16:16 + T], src[:, 16 - s:16 - s + T], ALU.add))
                    src, n, s = dst, 3 - n, 2 * s
                y = y_raw[:, i % 3]
                if i >= 3:
                    dve.wait_ge(yh_ok, i - 2)
                link(dve.tensor_tensor(y[:, 0:16], src[:, 16:32], cst[:, C_CNT + 16 * (i // 2):C_CNT + 16 * (i // 2) + 16], ALU.mult))
                dve.tensor_tensor(y[:, 0:16], y[:, 0:16], x[:, 16:32], ALU.subtract)
                dve.scalar_tensor_tensor(y[:, 16:T], src[:, 32:16 + T], 1.0 / w, x[:, 32:16 + T],
                                         ALU.mult, ALU.subtract).then_inc(y_ok, 1)
                dve.wait_ge(yh_ok, i + 1)
                low(y_lo[:, i], y, y_hi[:, i]).then_inc(yl_ok, 1)

            for i in range(4):
                pooled(i)
            link(mean_from(R_LNMEAN, ln_st, T, DA, 0.0))
            for i in range(NA):
                link(dve.tensor_tensor(v_fm[:, i], v_fm[:, i], ln_st[:, :], ALU.subtract))
                if i == 0:
                    link(dve.tensor_tensor(acc[:, :], v_fm[:, i], v_fm[:, i], ALU.mult))
                else:
                    link(dve.tensor_tensor(sq[:, :], v_fm[:, i], v_fm[:, i], ALU.mult))
                    link(dve.tensor_tensor(acc[:, :], acc[:, :], sq[:, :], ALU.add))
            dve.sem_inc(st_in, 1)
            for i in range(4, NA):
                pooled(i)
            rsqrt_from(R_LNVAR, 3, ln_st, T, DA)
            for i in range(NA):
                link(dve.tensor_tensor(v_fm[:, i], v_fm[:, i], ln_st[:, :], ALU.mult))
                dve.tensor_scalar(v_fm[:, i], v_fm[:, i], cst[:, C_LNG + i:C_LNG + i + 1],
                                  cst[:, C_LNB + i:C_LNB + i + 1], ALU.mult, ALU.add).then_inc(v_norm, 1)
            for i in range(NA):
                evacuated(U_IN + 2 * NA + i)
                dve.tensor_tensor(u_act[:, i], ps[i % 4][:, :], rms[:, :], ALU.mult).then_inc(u_ok, 1)
                dve.wait_ge(u_ok, i + 1)
                dve.sem_inc(evac, 1)
                if i == NA - 2:
                    dve.wait_ge(w_landed[U_SGU % 2], 16 * (U_SGU // 2 + 1))
                    later = w_raw[64:128, U_SGU % 2, 0:NA * P].rearrange("p (o i) -> p o i", i=P)
                    dve.memset(later[:, :, 0:64], 0.0).then_inc(sgu_masked, 1)
                if i == 3:
                    for n in range(2 * TT):
                        dve.wait_ge(vth_ok, n + 1)
                        t, c = n // 2, n % 2
                        low(vt_lo[:, t, c * 512:c * 512 + 512], ps[4 + n % 4][:, :],
                            vt_hi[:, t, c * 512:c * 512 + 512]).then_inc(vtl_ok, 1)
            for o in range(NA):
                dve.wait_ge(mv_hi, S_POOL + o + 1)
                low(a_lo[:, NA + o], ps[4 + o % 4][:, :], a_hi[:, NA + o], C_PSC + o).then_inc(mv_lo, 1)
            dve.wait_ge(bias_in, 16)
            dve.wait_ge(u_gelu, NA)
            for o in range(NA):
                dve.wait_ge(sgu_ps, o + 1)
                mixed = ps[4 + o % 4][:, :].rearrange("p (b i) -> p b i", b=TT)
                link(dve.tensor_tensor(sq[:, :].rearrange("p (b i) -> p b i", b=TT), mixed,
                                       bias_s[:, o:o + 1, :].to_broadcast([P, TT, P]), ALU.add))
                dve.tensor_tensor(u_act[:, o], u_act[:, o], sq[:, :], ALU.mult).then_inc(sgu_y, 1)
                dve.wait_ge(mv_hi, S_SGU + o + 1)
                low(a_lo[:, o], u_act[:, o], a_hi[:, o]).then_inc(mv_lo, 1)

            def residual(u0, n0):
                link(dve.memset(acc[:, :], 0.0))
                with dve.Fori(0, KT // 4) as r:
                    for k in range(4):
                        evacuated(r * 4 + (u0 + k))
                        hk = h[:, bass.ds(r * 4 + k, 1), :].rearrange("p a t -> p (a t)")
                        dve.tensor_tensor(hk, hk, ps[k][:, :], ALU.add).then_inc(h_ok, 1)
                        dve.wait_ge(h_ok, r * 4 + (n0 + k + 1))
                        dve.sem_inc(evac, 1)
                        dve.tensor_tensor(sq[:, :], hk, hk, ALU.mult).then_inc(hs_ok, 1)
                        dve.wait_ge(hs_ok, r * 4 + (n0 + k + 1))
                        dve.tensor_tensor(acc[:, :], acc[:, :], sq[:, :], ALU.add).then_inc(acc_ok, 1)
                dve.wait_ge(acc_ok, n0 + KT)
                dve.sem_inc(st_in, 1)

            dve.wait_ge(x_back, 16)
            residual(U_OUT, 0)
            for k in range(KT):
                dve.wait_ge(mv_hi, S_N2 + k + 1)
                low(a_lo[:, k], h[:, k], a_hi[:, k], C_GX + k).then_inc(mv_lo, 1)
            rsqrt_from(R_N2, 4, rms, T, D)
            with dve.Fori(0, KT // 4) as r:
                for k in range(4):
                    evacuated(r * 4 + (U_WQ + k))
                    dve.tensor_tensor(q_raw[:, bass.ds(r * 4 + k, 1), :].rearrange("p a t -> p (a t)"),
                                      ps[k][:, :], rms[:, :], ALU.mult).then_inc(q_ok, 1)
                    dve.wait_ge(q_ok, r * 4 + (k + 1))
                    dve.sem_inc(evac, 1)
            for k in range(KT):
                dve.wait_ge(mv_hi, S_Q + k + 1)
                low(a_lo[:, k], q_raw[:, k], a_hi[:, k]).then_inc(mv_lo, 1)

            def maxima(head):
                dve.wait_ge(sc_ps, head + 1)
                for b in range(2):
                    link(dve.tensor_reduce(stat[:, 0, head, 2 * b:2 * b + 2],
                                           ps[4 + 2 * (head % 2) + b][:, :].rearrange("p (t m) -> p t m", t=2), AX, ALU.max))
                dve.tensor_scalar(stat[:, 0, head], stat[:, 0, head], -SCALE, None, ALU.mult).then_inc(mx_ok, 1)

            def normalised(head):
                dve.wait_ge(ex_ok, TT * (head + 1))
                link(dve.reciprocal(stat[:, 2, head], stat[:, 1, head]))
                pr = prob[:, head % 2]
                dve.tensor_tensor(pr, pr, stat[:, 2, head].rearrange("p (t a) -> p t a", a=1).to_broadcast([P, TT, M]),
                                  ALU.mult).then_inc(pn_ok, 1)

            maxima(0)
            normalised(0)
            for head in range(XH):
                for m in range(MT):
                    dve.wait_ge(pth_ok, MT * head + m + 1)
                    low(pt_lo[:, head % 2, m], ps[m][:, :], pt_hi[:, head % 2, m]).then_inc(ptl_ok, 1)
                if head + 1 < XH:
                    maxima(head + 1)
                for n in range(HT):
                    if head + 1 < XH and n == 2:
                        normalised(head + 1)
                    o = head * HT + n
                    dve.wait_ge(mv_hi, S_O + o + 1)
                    low(a_lo[:, o], ps[2 + o % 2][:, :], a_hi[:, o]).then_inc(mv_lo, 1)
            dve.wait_ge(keyh_ok, 1)
            low(key_lo[:, :, :], key_raw[:, :, :], key_hi[:, :, :]).then_inc(keyl_ok, 1)

            residual(U_WO, KT)
            rsqrt_from(R_N3, 5, rms, T, D)
            dve.wait_ge(keyl_ok, 1)
            for k in range(KT):
                dve.scalar_tensor_tensor(q_raw[:, k], h[:, k], cst[:, C_GPEER + k:C_GPEER + k + 1], rms[:, :],
                                         ALU.mult, ALU.mult).then_inc(h_ok, 1)
                if k:
                    dve.wait_ge(mv_hi, S_N3 + k)
                    low(a_lo[:, k - 1], q_raw[:, k - 1], a_hi[:, k - 1]).then_inc(mv_lo, 1)
            dve.wait_ge(mv_hi, S_N3 + KT)
            low(a_lo[:, KT - 1], q_raw[:, KT - 1], a_hi[:, KT - 1]).then_inc(mv_lo, 1)

            with dve.Fori(0, KT // 4) as r:
                for k in range(4):
                    dve.wait_ge(qyh_ok, r * 4 + (k + 1))
                    low(qy_lo[:, k % 2], ps[k][:, :], qy_hi[:, k % 2]).then_inc(evac, 1)

            PER = 18
            dve.wait_ge(qs_ok, BANKS + KT)

            with dve.Fori(0, TT) as t:
                n = [0]

                def step(ins):
                    n[0] += 1
                    ins.then_inc(tk, 1)
                    dve.wait_ge(tk, t * PER + n[0])
                    dve.sem_inc(tk_seen, 1)

                def top16(vals, idx, src, rest, count):
                    for c in range(count):
                        last = dve.max(vals[:, c, 0:8], src[:, c])
                    step(last)
                    for c in range(count):
                        last = dve.match_replace(rest[:, c], vals[:, c, 0:8], src[:, c], LOWEST)
                    step(last)
                    for c in range(count):
                        last = dve.max(vals[:, c, 8:16], rest[:, c])
                    step(last)
                    for c in range(count):
                        dve.max_index(idx[:, c, 0:8], vals[:, c, 0:8], src[:, c])
                        last = dve.max_index(idx[:, c, 8:16], vals[:, c, 8:16], rest[:, c])
                    step(last)

                step(dve.tensor_copy(s_w[:, :, :], score[:, bass.ds(t, 1)].rearrange("p a h n -> p (a h) n")))
                top16(top_v, top_i, s_w, s_w2, HP)
                dve.tensor_copy(top_f[:, :, :], top_i[:, :, :])
                halves = top_v[:, :, :].rearrange("p (h s) k -> p h s k", s=2)
                for c in range(PH):
                    last = dve.tensor_tensor(cand[:, c].rearrange("p (a b) -> p a b", a=16),
                                             halves[:, c, 0].rearrange("p (a b) -> p a b", b=1).to_broadcast([P, 16, 16]),
                                             halves[:, c, 1:2].to_broadcast([P, 16, 16]), ALU.add)
                step(last)
                top16(best, pos, cand, cand2, PH)
                flat = pos[:, :, :].rearrange("p h k -> p (h k)")
                dve.tensor_scalar(pos_ab[:, 0], flat, 4, None, ALU.logical_shift_right)
                step(dve.tensor_scalar(pos_ab[:, 1], flat, 15, None, ALU.bitwise_and))
                dve.tensor_tensor(pick[:, 2, bass.ds(t, 1)].rearrange("p a (h k) -> p (a h) k", h=PH), best[:, :, :],
                                  best[:, :, 0:1].to_broadcast([P, PH, 16]), ALU.subtract)
                step(dve.tensor_copy(pos_f[:, :, :], pos_ab[:, :, :]))
                for s in range(2):
                    step(dve.tensor_tensor(match[:, :, :],
                                           pos_f[:, s].rearrange("p (n a) -> p n a", a=1).to_broadcast([P, HK, 16]),
                                           cst[:, C_IOTA:C_IOTA + 16].rearrange("p (a n) -> p a n", a=1).to_broadcast([P, HK, 16]),
                                           ALU.is_equal))
                    for c in range(PH):
                        m = match[:, c * TOPK:(c + 1) * TOPK, :]
                        last = dve.tensor_tensor(m, m, top_f[:, 2 * c + s:2 * c + s + 1, :].to_broadcast([P, TOPK, 16]), ALU.mult)
                    step(last)
                    step(dve.tensor_reduce(pick[:, s, bass.ds(t, 1)].rearrange("p a n -> p (a n)"), match[:, :, :],
                                           AX, ALU.add))
                assert n[0] == PER, n[0]
            dve.sem_inc(gexp_in, 1)
            dve.wait_ge(gexp_ok, 1)
            soft = pick[:, 2].rearrange("p t (h k) -> p (t h) k", k=TOPK)
            link(dve.tensor_reduce(gsum[:, 0], soft, AX, ALU.add))
            link(dve.reciprocal(gsum[:, 1], gsum[:, 0]))
            dve.tensor_tensor(soft, soft, gsum[:, 1].rearrange("p (n a) -> p n a", a=1).to_broadcast([P, TT * PH, TOPK]),
                              ALU.mult).then_inc(pick_ok, 1)
            dve.wait_ge(h_out, 16)
            dve.wait_ge(pick_ps, 1)
            dve.tensor_copy(i_T[:, :], ps[4][:, :]).then_inc(idx_ok, 1)
            dve.tensor_copy(j_T[:, :], ps[5][:, :]).then_inc(idx_ok, 1)
            dve.tensor_copy(gt_hi[:, :], ps[6][:, :]).then_inc(idx_ok, 1)
            dve.wait_ge(idx_ok, 3)
            low(gt_lo[:, :], ps[6][:, :], gt_hi[:, :]).then_inc(idx_ok, 1)
            dve.wait_ge(idx_ok, 4)
            def one_hots(b, n):
                slot = n % 2
                for w in range(4):
                    tok = b * 4 + (4 * n + w)
                    col = slice(tok, tok + 1) if isinstance(b, int) else bass.ds(tok, 1)
                    x = 4 * slot + w
                    dve.tensor_scalar(oh_j[:, x], iota, j_T[:, col], None, ALU.is_equal)
                    dve.tensor_scalar(oh_i[:, x, 0], iota, i_T[:, col], gt_hi[:, col].bitcast(F32),
                                      ALU.is_equal, ALU.mult)
                    last = dve.tensor_scalar(oh_i[:, x, 1], iota, i_T[:, col], gt_lo[:, col].bitcast(F32),
                                             ALU.is_equal, ALU.mult)
                last.then_inc(oh_ok, 1)

            def gate_sum(b, n, slot, col):
                dve.wait_ge(g_ps, b + (n + 1))
                for x in range(2):
                    last = dve.tensor_reduce(g_out[:, slot, :, bass.ds(col + 2 * x, 2)].rearrange("p i t -> p t i"),
                                             ps[4 + 2 * (n % 2) + x][:, :].rearrange("p (t s i) -> p t i s", t=2, s=2),
                                             AX, ALU.add)
                last.then_inc(g_ok, 1)

            STEPS = G_TOK // 4

            def gate_sums(q, slot, pairs):
                if not (isinstance(q, int) and q == 0):
                    dve.wait_ge(g_st[slot], q * 16)
                    dve.sem_inc(tk_seen, 1)
                with dve.Fori(0, pairs) as x:
                    for n in range(2):
                        gate_sum(q * (2 * STEPS) + x * 2 + slot * STEPS, n, slot, x * 8 + 4 * n)
                        one_hots(q * (2 * STEPS) + x * 2 + slot * STEPS, n + 2)

            for n in range(2):
                one_hots(0, n)
            q_last = T // G_TOK // 2 - 1
            for slot in range(2):
                gate_sums(0, slot, STEPS // 2)
            with dve.Fori(1, q_last) as q:
                for slot in range(2):
                    gate_sums(q, slot, STEPS // 2)
            gate_sums(q_last, 0, STEPS // 2)
            gate_sums(q_last, 1, STEPS // 2 - 1)
            for n in range(2):
                gate_sum(T // 4 - 2, n, 1, G_TOK - 8 + 4 * n)

            def product(m, n):
                s = n // 4
                if n % 4 == 0:
                    dve.wait_ge(ag_in[s], m * 32 + 32)
                a = a_in[:, s, n % 4].rearrange("p (b t) -> p b t", t=G_TOK)
                dve.tensor_tensor(a, a, g_in[:, s, :, n % 4], ALU.mult).then_inc(am_ok, 1)

            def gated_low(m, buf, n):
                dve.wait_ge(ah_ok, m * EG + (n + 1))
                low(ga_lo[:, buf, n], a_in[:, n // 4, n % 4], ga_hi[:, buf, n]).then_inc(al_ok, 1)

            for n in range(EG):
                product(0, n)
            for n in range(EG):
                gated_low(0, 0, n)
            for n in range(BANKS):
                dve.wait_ge(ea_ok, ET + n + 1)
                dve.sem_inc(add_ok, 1)
            dve.wait_ge(h_back, 32)

            def v_group(g2, b, prep=True, squares=False):
                for c in range(DC):
                    if prep:
                        product(g2 * 2 + (b + 1), c)
                        gated_low(g2 * 2 + (b + 1), 1 - b, c)
                    dve.wait_ge(unit_done, g2 * (2 * DC) + (U_EV + b * DC + c + 1))
                    for d in range(2):
                        k = 2 * c + d
                        dve.tensor_tensor(h[:, k], h[:, k], ps[k % 4][:, :], ALU.add).then_inc(add_ok, 1)
                    if squares:
                        for k in (2 * c, 2 * c + 1):
                            dve.wait_ge(add_ok, BANKS + KT * (NG - 1) + 2 * c + 2)
                            t = acc if k == 0 else sq
                            link(dve.tensor_tensor(t[:, :], h[:, k], h[:, k], ALU.mult))
                            if k:
                                link(dve.tensor_tensor(acc[:, :], acc[:, :], sq[:, :], ALU.add))

            with dve.Fori(0, NG // 2 - 1) as g2:
                v_group(g2, 0)
                v_group(g2, 1)
            v_group(NG // 2 - 1, 0)
            v_group(NG // 2 - 1, 1, prep=False, squares=True)
            dve.sem_inc(st_in, 1)
            rsqrt_from(R_FIN, 6, rms, T, D)
            for k in range(KT):
                dve.scalar_tensor_tensor(h[:, k], h[:, k], cst[:, C_GFIN + k:C_GFIN + k + 1], rms[:, :],
                                         ALU.mult, ALU.mult).then_inc(o_ok, 1)

        @block.tensor
        def _(pe):
            def three(out, wh, wl, mh, ml, start, stop):
                pe.matmul(out, wh, mh, start=start, stop=False)
                pe.matmul(out, wh, ml, start=False, stop=False)
                return pe.matmul(out, wl, mh, start=False, stop=stop)

            def unit(u, s, bank, hi, lo, cols, pidx, moving=None, order=range(KT), done=evac, mid=None, half=None):
                pe.wait_ge(done, pidx + 1)
                for n, k in enumerate(order):
                    if n == 8 and mid is not None:
                        mid()
                    if n % 8 == 0:
                        pe.wait_ge(w_lo_ok, u * 2 + (k // 8 + 1))
                    if moving is not None:
                        pe.wait_ge(mv_lo, moving + n + 1)
                    w = slice(k * P, (k + 1) * P)
                    ins = three(ps[bank][:, 0:cols], w_hi[:, s, w], w_lo[:, s, w],
                                hi[:, k, 0:cols], lo[:, k, 0:cols], n == 0, n == KT - 1)
                    if n == 7 and half is not None:
                        ins.then_inc(half, 1)
                ins.then_inc(unit_done, 1)

            def units(u0, n, hi, lo, cols, pidx, moving, order=range(KT)):
                with pe.Fori(0, n // 4) as r:
                    for k in range(4):
                        unit(r * 4 + (u0 + k), (u0 + k) % 2, k, hi, lo, cols, r * 4 + (pidx + k),
                             moving if k == 0 else None, order)

            def total(n, cols):
                pe.wait_ge(st_in, n + 1)
                pe.matmul(ps[7][:, 0:cols], ones, acc[:, 0:cols], start=True, stop=True).then_inc(st_ps, 1)

            pe.wait_ge(cst_in, 16)
            for k in range(4):
                unit(U_KV + k, k % 2, k, m_hi, m_lo, M, k, S_MEM if k == 0 else None)
                if k == 2:
                    total(R_MEM, M)
            with pe.Fori(1, KT // 4) as r:
                for k in range(4):
                    unit(r * 4 + (U_KV + k), k % 2, k, m_hi, m_lo, M, r * 4 + k)
            def v_transpose(r, k):
                pe.wait_ge(kv_ok, r * 4 + (KT + k + 1))
                pe.wait_ge(kvl_ok, r * 4 + (KT - 4 + k + 1))
                for m in range(MT):
                    ins = pe.transpose(ps[4 + k][:, m * P:(m + 1) * P], kv_raw[:, k, m * P:(m + 1) * P], ident)
                ins.then_inc(vT_ok, 1)

            pe.wait_ge(st_ms, 1)
            with pe.Fori(0, XH) as r:
                for k in range(HT):
                    unit(r * 4 + (U_KV + KT + k), k % 2, k, m_hi, m_lo, M, r * 4 + (KT + k),
                         mid=(lambda: v_transpose(r, k - 1)) if k else None)
                v_transpose(r, HT - 1)
            def x_total():
                pe.wait_ge(kvl_ok, 2 * KT)
                total(R_X, T)

            p0 = 2 * KT
            for i in range(NA):
                unit(U_IN + i, i % 2, i % 4, a_hi, a_lo, T, p0 + i, S_X if i == 0 else None,
                     mid=x_total if i == 0 else None)
            for i in range(NA):
                unit(U_IN + NA + i, i % 2, i % 4, a_hi, a_lo, T, p0 + NA + i)
                if i == 2:
                    total(R_LNMEAN, T)
                if i == NA - 1:
                    total(R_LNVAR, T)
            for i in range(NA):
                unit(U_IN + 2 * NA + i, i % 2, i % 4, a_hi, a_lo, T, p0 + 2 * NA + i)
                if i == 3:
                    pe.wait_ge(v_norm, NA)
                    for n in range(2 * TT):
                        t, c = n // 2, n % 2
                        if n >= 4:
                            pe.wait_ge(vtl_ok, n - 3)
                        for x in range(4):
                            ins = pe.transpose(ps[4 + n % 4][:, x * P:(x + 1) * P],
                                               v_fm[:, 4 * c + x, t * P:(t + 1) * P], ident)
                        ins.then_inc(vtt_ok, 1)
            pe.wait_ge(w_lo_ok, 2 * U_POOL + 2)
            pe.wait_ge(yl_ok, NA)
            pe.wait_ge(vtl_ok, 2 * TT)
            for o in range(NA):
                g = o // 2
                if o >= 4:
                    pe.wait_ge(mv_lo, S_POOL + o - 3)
                for c in range(2):
                    at_w = (g * 2 + c) * 256 + (o % 2) * P
                    s = U_POOL % 2
                    ins = three(ps[4 + o % 4][:, :], w_hi[:, s, at_w:at_w + P], w_lo[:, s, at_w:at_w + P],
                                y_hi[:, 2 * g + c], y_lo[:, 2 * g + c], c == 0, c == 1)
                ins.then_inc(pool_ps, 1)
            pe.wait_ge(pool_ps, NA)
            pe.sem_inc(unit_done, 1)
            pe.wait_ge(w_lo_ok, 2 * U_SGU + 2)
            s = U_SGU % 2
            for o in range(NA):
                pe.wait_ge(mv_lo, S_POOL + NA - 3 + o if o < 4 else S_SGU + o - 3)
                f = slice(o * P, (o + 1) * P)
                for b in range(TT):
                    ins = three(ps[4 + o % 4][:, b * P:(b + 1) * P], vt_hi[:, b, f], vt_lo[:, b, f],
                                w_hi[:, s, f], w_lo[:, s, f], True, True)
                ins.then_inc(sgu_ps, 1)
            pe.wait_ge(sgu_ps, NA)
            pe.sem_inc(unit_done, 1)

            p0 += 3 * NA
            units(U_OUT, KT, a_hi, a_lo, T, p0, S_POOL, order=[*range(NA, KT), *range(NA)])
            p0 += KT

            def units_with_total(u0, p0, moving, n):
                for k in range(4):
                    unit(u0 + k, k % 2, k, a_hi, a_lo, T, p0 + k, moving if k == 0 else None)
                    if k == 0:
                        total(n, T)
                with pe.Fori(1, KT // 4) as r:
                    for k in range(4):
                        unit(r * 4 + (u0 + k), k % 2, k, a_hi, a_lo, T, r * 4 + (p0 + k))

            units_with_total(U_WQ, p0, S_N2, R_N2)
            p0 += KT

            def scores(head):
                s = head % 2
                pe.wait_ge(k_land[s], 16 * (head // 2 + 1))
                if head >= 2:
                    pe.wait_ge(ex_ok, TT * (head - 1))
                for t in range(TT):
                    for n in range(HT):
                        k = head * HT + n
                        if t == 0:
                            pe.wait_ge(mv_lo, S_Q + k + 1)
                        tok = slice(t * P, (t + 1) * P)
                        ins = three(ps[4 + 2 * s + t // 2][:, (t % 2) * M:(t % 2 + 1) * M], a_hi[:, k, tok], a_lo[:, k, tok],
                                    k_in[:, s, 0, n], k_in[:, s, 1, n], n == 0, n == HT - 1)
                ins.then_inc(sc_ps, 1)

            pe.wait_ge(evac, BANKS + p0)
            scores(0)
            scores(1)
            def prob_transpose(head):
                pe.wait_ge(pn_ok, head + 1)
                if head:
                    pe.wait_ge(ptl_ok, MT * head)
                for m in range(MT):
                    for t in range(TT):
                        ins = pe.transpose(ps[m][:, t * P:(t + 1) * P], prob[:, head % 2, t, m * P:(m + 1) * P], ident)
                ins.then_inc(pT_ps, 1)

            prob_transpose(0)
            for head in range(XH):
                s = head % 2
                pe.wait_ge(v_land[s], 16 * (head // 2 + 1))
                pe.wait_ge(ptl_ok, MT * (head + 1))
                for n in range(HT):
                    o = head * HT + n
                    if o >= 2:
                        pe.wait_ge(mv_lo, S_O + o - 1)
                    f = slice(n * P, (n + 1) * P)
                    for m in range(MT):
                        ins = three(ps[2 + o % 2][:, :], v_in[:, s, 0, m, f], v_in[:, s, 1, m, f],
                                    pt_hi[:, s, m], pt_lo[:, s, m], m == 0, m == MT - 1)
                    ins.then_inc(o_ps, 1)
                if head + 1 < XH:
                    prob_transpose(head + 1)
                if head + 2 < XH:
                    scores(head + 2)
            pe.wait_ge(mv_lo, S_O + KT)
            units(U_WO, KT, a_hi, a_lo, T, p0, S_O)
            p0 += KT
            total(R_N3, T)
            pe.wait_ge(keyl_ok, 1)
            pe.wait_ge(st_ms, 5)
            pe.sem_inc(qs_ps, 3)

            def query_scores(r, k):
                pe.wait_ge(evac, r * 4 + (p0 + k + 1 + BANKS))
                pe.wait_ge(qs_ok, r * 4 + (k + 1))
                kk = bass.ds(r * 4 + k, 1)
                mh = key_hi[:, kk, :].rearrange("p a n -> p (a n)")
                ml = key_lo[:, kk, :].rearrange("p a n -> p (a n)")
                for t in range(TT):
                    tok = slice(t * P, (t + 1) * P)
                    out = ps[4 + k % 4][:, tok]
                    ins = three(out, qy_hi[:, k % 2, tok], qy_lo[:, k % 2, tok], mh, ml, True, True)
                ins.then_inc(qs_ps, 1)

            def query_round(r, first=False):
                for k in range(4):
                    unit(r * 4 + (U_QY + k), k % 2, k, a_hi, a_lo, T, r * 4 + (p0 + k), S_N3 if first and k == 0 else None,
                         mid=None if first and k == 0 else (lambda: query_scores(r, k - 1)))

            query_round(0, True)
            with pe.Fori(1, KT // 4) as r:
                query_round(r)

            pe.wait_ge(evac, BANKS + p0 + KT - 3)

            def u_round(r, beside=None, half=None):
                for k in range(4):
                    unit(r * 4 + (U_EU + k), k % 2, k, a_hi, a_lo, T, r * 4 + k, done=ea_ok,
                         mid=beside and (lambda: beside(2 * k)), half=half if k == 3 else None)
                    if beside:
                        beside(2 * k + 1)

            def last_scores(n):
                if n == 0:
                    query_scores(KT // 4, -1)

            def choices(n):
                if n == 2:
                    pe.wait_ge(qs_ok, BANKS + KT)
                    pe.wait_ge(pick_ok, 1)
                    for m in range(3):
                        for t in range(TT):
                            ins = pe.transpose(ps[4 + m][:, t * P:(t + 1) * P], pick[:, m, t], ident)
                    ins.then_inc(pick_ps, 1)

            u_round(0, last_scores)
            with pe.Fori(1, G_LEAD - 1) as r:
                u_round(r)
            u_round(G_LEAD - 1, choices)
            pe.wait_ge(idx_ok, 4)

            def gates(b, n, first):
                pe.wait_ge(oh_ok, b + (n + 1))
                if not first:
                    pe.wait_ge(g_ok, b + (n - 1))
                for w in range(4):
                    x = 4 * (n % 2) + w
                    out = ps[4 + 2 * (n % 2) + w // 2][:, (w % 2) * 2 * P:(w % 2 + 1) * 2 * P]
                    ins = pe.matmul(out, oh_j[:, x], oh_i[:, x].rearrange("p s i -> p (s i)"), start=True, stop=True)
                ins.then_inc(g_ps, 1)

            def g_rounds(q):
                for part in range(4):
                    u_round(q * 4 + (G_LEAD + part),
                            lambda n: gates(q * 32 + part * 8, n, isinstance(q, int) and q == 0 and part == 0 and n < 2))

            g_rounds(0)
            with pe.Fori(1, G_ROUNDS // 4) as q:
                g_rounds(q)
            with pe.Fori(G_LEAD + G_ROUNDS, ET // 4 - 1) as r:
                u_round(r)
            u_round(ET // 4 - 1, half=n3_half)

            def v_group(g2, b):
                for c in range(DC):
                    u = g2 * (2 * DC) + (U_EV + b * DC + c)
                    s = c % 2
                    pe.wait_ge(w_lo_ok, u * 2 + 2)
                    for d in range(2):
                        pe.wait_ge(add_ok, g2 * (2 * KT) + (b * KT + 2 * c + d + 1))
                        for n in range(EG):
                            if c == 0 and d == 0:
                                pe.wait_ge(al_ok, g2 * (2 * EG) + (b * EG + n + 1))
                            w = slice(n * 256 + d * P, n * 256 + (d + 1) * P)
                            ins = three(ps[(2 * c + d) % 4][:, :], w_hi[:, s, w], w_lo[:, s, w],
                                        ga_hi[:, b, n], ga_lo[:, b, n], n == 0, n == EG - 1)
                    ins.then_inc(unit_done, 1)

            with pe.Fori(0, NG // 2) as g2:
                v_group(g2, 0)
                v_group(g2, 1)
            total(R_FIN, T)


def _units(w):
    n = w.shape[1] // P
    return w.reshape(KT, P, n, P).transpose(2, 1, 0, 3).reshape(n, P, KT * P)


def _cols(v):
    return v.reshape(-1, P).T


def kernel(x, mem, g_mix, w_in, sgu_ln_g, sgu_ln_b, sgu_w, sgu_b, pool_w, pool_scale, w_out,
           g_xattn, g_mem, xattn_w_q, xattn_w_kv, xattn_w_o,
           g_peer, peer_w_query, peer_sub_keys, peer_u, peer_v, g_final):
    import numpy as np
    import concourse.bacc as bacc
    from concourse.bass_utils import run_bass_kernel_spmd

    def arr(a):
        return np.asarray(a)

    w = np.zeros((N_UNITS, P, 2048), np.float32)
    w[U_KV:U_IN] = _units(arr(xattn_w_kv)[0])
    win = _units(arr(w_in)[0])
    w[U_IN:U_IN + 2 * NA] = win[NA:]
    w[U_IN + 2 * NA:U_POOL] = win[:NA]
    w[U_POOL] = arr(pool_w)[0].reshape(4, 2, P, 256).transpose(2, 0, 1, 3).reshape(P, 2048)
    w[U_SGU, :, :NA * P] = arr(sgu_w)[0].transpose(2, 0, 1).reshape(P, NA * P)
    w[U_OUT:U_WQ] = _units(arr(w_out)[0])
    w[U_WQ:U_WO] = _units(arr(xattn_w_q)[0])
    w[U_WO:U_QY] = _units(arr(xattn_w_o)[0])
    w[U_QY:U_EU] = _units(arr(peer_w_query)[0])
    w[U_EU:U_EV] = arr(peer_u)[0].reshape(ET, P, KT, P).transpose(0, 3, 2, 1).reshape(ET, P, 2048)
    w[U_EV:] = arr(peer_v)[0].reshape(NG, EG, P, DC, 256).transpose(0, 3, 2, 1, 4).reshape(NG * DC, P, 2048)

    tokens = np.arange(16)
    counts = np.stack([1.0 / np.minimum(tokens + 1, w_) for w_ in (2, 4, 8, 16)]).astype(np.float32)
    const = np.concatenate([
        _cols(arr(g_mix)[0]), _cols(arr(g_xattn)[0]), _cols(arr(g_mem)[0]), _cols(arr(g_peer)[0]), _cols(arr(g_final)),
        _cols(arr(sgu_ln_g)[0]), _cols(arr(sgu_ln_b)[0]), _cols(arr(pool_scale)[0]),
        np.broadcast_to(counts.reshape(1, 64), (P, 64)), np.eye(P, dtype=np.float32), np.ones((P, P), np.float32),
        np.broadcast_to(np.arange(P, dtype=np.float32), (P, P)),
    ], axis=1)
    arrays = {
        "weights": w,
        "x_t": arr(x)[0].T.reshape(KT, P, T).transpose(1, 0, 2),
        "mem_t": arr(mem)[0].T.reshape(KT, P, M).transpose(1, 0, 2),
        "constants": const,
        "sgu_bias": np.broadcast_to(arr(sgu_b)[0][None], (P, NA, P)),
        "sub_keys": arr(peer_sub_keys)[0].reshape(HP, NK, P).transpose(2, 0, 1),
    }
    arrays = {name: np.ascontiguousarray(a) for name, a in arrays.items()}
    nc = bacc.Bacc("TRN2", target_bir_lowering=False, num_devices=1, dynamic_dma_scratch_size=1024)
    ins = [nc.dram_tensor(name, a.shape, F32, kind="ExternalInput").ap() for name, a in arrays.items()]
    out = nc.dram_tensor("out_t", (P, KT, T), F32, kind="ExternalOutput").ap()
    hybrid_block(nc, *ins, out)
    r = run_bass_kernel_spmd(nc, [arrays], core_ids=[0])
    return r.results[0]["out_t"].transpose(1, 0, 2).reshape(D, T).T.reshape(1, T, D).copy()
```
